# Optimizing a Trainium2 kernel written in Bass

```python
import math
import jax
import jax.numpy as jnp
from jax import lax
import numpy as np

D_MODEL = 1024
BATCH = 1
SEQ = 512
DEPTH = 1
DEC_BATCH = 8
DEC_SEQ = 4
PAST_LEN = 1024
PAGE_SIZE = 128

HEAD_DIM = 64
ATTN_WIDTH = D_MODEL // 2
N_HEADS = ATTN_WIDTH // HEAD_DIM
N_KV = 2
GROUP = N_HEADS // N_KV
KV_WIDTH = N_KV * HEAD_DIM
CONV_WIDTH = D_MODEL - ATTN_WIDTH
CONV_K = 31
CMP_LEN = 32
CMP_STRIDE = 16
CMP_HIDDEN = 256
SEL_BLOCK = 64
TOP_N = 16
WINDOW = 512
N_BUCKETS = 32
MAX_DISTANCE = 128
Q_BLOCK = 64
PEER_HEADS = 8
PEER_DQ = 256
N_KEYS = 128
N_EXPERTS = N_KEYS * N_KEYS
PEER_TOPK = 16
PEER_BLOCK = 256
FORCE_SCORE = 1.0e4
EPS = 1e-6
SPLIT_SIZES = (ATTN_WIDTH, KV_WIDTH, KV_WIDTH, KV_WIDTH, KV_WIDTH, KV_WIDTH, KV_WIDTH, 3 * N_HEADS, 2 * CONV_WIDTH)
IN_COLS = sum(SPLIT_SIZES)

kernel_name = 'hymba_nsa_conformer_peer_step'

def rms_norm(x, g):
    xf = x.astype(jnp.float32)
    y = xf * lax.rsqrt(jnp.mean(xf * xf, axis=-1, keepdims=True) + EPS)
    return (y * g.astype(jnp.float32)).astype(x.dtype)

def layer_norm(x, g, b):
    xf = x.astype(jnp.float32)
    mu = jnp.mean(xf, axis=-1, keepdims=True)
    var = jnp.mean(jnp.square(xf - mu), axis=-1, keepdims=True)
    y = (xf - mu) * lax.rsqrt(var + EPS) * g.astype(jnp.float32) + b.astype(jnp.float32)
    return y.astype(x.dtype)

def masked_softmax(logits, mask, axis):
    neg = jnp.where(mask, logits, -jnp.inf)
    m = jnp.max(neg, axis=axis, keepdims=True)
    m = jnp.where(jnp.isfinite(m), m, 0.0)
    e = jnp.where(mask, jnp.exp(neg - m), 0.0)
    d = jnp.sum(e, axis=axis, keepdims=True)
    return e / jnp.where(d > 0.0, d, 1.0)

def t5_bucket(dist):
    n = jnp.maximum(dist, 0)
    exact = N_BUCKETS // 2
    nf = jnp.maximum(n, 1).astype(jnp.float32)
    large = exact + (jnp.log(nf / exact) / math.log(MAX_DISTANCE / exact) * (N_BUCKETS - exact)).astype(jnp.int32)
    return jnp.where(n < exact, n, jnp.minimum(large, N_BUCKETS - 1))

def compress(rows, pe, w1, b1, w2, b2):
    B, L = rows.shape[0], rows.shape[1]
    ratio = CMP_LEN // CMP_STRIDE
    n_chunks = L // CMP_STRIDE
    nc = n_chunks - ratio + 1
    r = rows[:, :n_chunks * CMP_STRIDE].reshape(B, n_chunks, CMP_STRIDE, N_KV, HEAD_DIM)
    w1c = w1.reshape(ratio, CMP_STRIDE, HEAD_DIM, CMP_HIDDEN)
    parts = jnp.einsum('bcsgd,jsdh->jbcgh', r, w1c)
    hid = b1 + pe.reshape(-1) @ w1
    for j in range(ratio):
        hid = hid + parts[j, :, j:j + nc]
    out = jax.nn.gelu(hid) @ w2 + b2
    end = jnp.arange(nc, dtype=jnp.int32) * CMP_STRIDE + (CMP_LEN - 1)
    return out, end

def compress_branch(rows, lp, which):
    return compress(rows, lp['cmp_pe'][which], lp['cmp_w1'][which], lp['cmp_b1'][which],
                    lp['cmp_w2'][which], lp['cmp_b2'][which])

def to_blocks(rows):
    B, L = rows.shape[0], rows.shape[1]
    ns = -(-L // SEL_BLOCK)
    rows = jnp.pad(rows, ((0, 0), (0, ns * SEL_BLOCK - L), (0, 0), (0, 0)))
    return jnp.transpose(rows.reshape(B, ns, SEL_BLOCK, N_KV, HEAD_DIM), (0, 3, 1, 2, 4))

def nsa_block(q, t_pos, gates, kc, vc, kc_end, ks_blk, vs_blk, kw, vw, w_pos, rel_bias):
    B = q.shape[0]
    scale = HEAD_DIM ** -0.5
    tbl = rel_bias.astype(jnp.float32).reshape(N_BUCKETS, N_KV, GROUP)
    lc = jnp.einsum('bqgrd,bcgd->bqgrc', q, kc).astype(jnp.float32) * scale
    dc = t_pos[:, None] - kc_end[None, :]
    lc = lc + jnp.transpose(tbl[t5_bucket(dc)], (0, 2, 3, 1))[None]
    pc = masked_softmax(lc, (dc >= 0)[None, :, None, None, :], axis=-1)
    o_cmp = jnp.einsum('bqgrc,bcgd->bqgrd', pc.astype(vc.dtype), vc)
    nc, ns = kc.shape[1], ks_blk.shape[2]
    ci = jnp.arange(nc)[:, None]
    sj = jnp.arange(ns)[None, :]
    cover = ((ci * CMP_STRIDE < (sj + 1) * SEL_BLOCK) & (ci * CMP_STRIDE + CMP_LEN > sj * SEL_BLOCK)).astype(jnp.float32)
    imp = jnp.einsum('bqgrc,cj->bqgj', pc, cover)
    cur = (t_pos // SEL_BLOCK)[:, None]
    forced = (sj == 0) | (sj == cur) | (sj == cur - 1)
    valid = sj * SEL_BLOCK <= t_pos[:, None]
    imp = jnp.where(forced[None, :, None, :], imp + FORCE_SCORE, imp)
    imp = jnp.where(valid[None, :, None, :], imp, -FORCE_SCORE)
    _, idx = lax.top_k(imp, min(TOP_N, ns))
    bi = jnp.arange(B)[:, None, None, None]
    gi = jnp.arange(N_KV)[None, None, :, None]
    ks_g = ks_blk[bi, gi, idx]
    vs_g = vs_blk[bi, gi, idx]
    ls = jnp.einsum('bqgrd,bqgnkd->bqgrnk', q, ks_g).astype(jnp.float32) * scale
    pos = idx[..., None] * SEL_BLOCK + jnp.arange(SEL_BLOCK, dtype=jnp.int32)
    ds = t_pos[None, :, None, None, None] - pos
    tblk = jnp.transpose(tbl, (1, 0, 2))
    bs = tblk[jnp.arange(N_KV)[None, None, :, None, None], t5_bucket(ds)]
    ls = ls + jnp.moveaxis(bs, -1, 3)
    ps = masked_softmax(ls, (ds >= 0)[:, :, :, None], axis=(-2, -1))
    o_sel = jnp.einsum('bqgrnk,bqgnkd->bqgrd', ps.astype(vs_g.dtype), vs_g)
    lw = jnp.einsum('bqgrd,bwgd->bqgrw', q, kw).astype(jnp.float32) * scale
    dw = t_pos[:, None] - w_pos[None, :]
    lw = lw + jnp.transpose(tbl[t5_bucket(dw)], (0, 2, 3, 1))[None]
    mw = (dw >= 0) & (dw < WINDOW) & (w_pos >= 0)[None, :]
    pw = masked_softmax(lw, mw[None, :, None, None, :], axis=-1)
    o_win = jnp.einsum('bqgrw,bwgd->bqgrd', pw.astype(vw.dtype), vw)
    return gates[..., 0:1] * o_cmp + gates[..., 1:2] * o_sel + gates[..., 2:3] * o_win

def nsa_prompt(q, gates, kc_raw, vc_raw, ks, vs, kw, vw, lp, rel_bias):
    B, T = q.shape[0], q.shape[1]
    kc, kc_end = compress_branch(kc_raw, lp, 0)
    kc = rms_norm(kc, lp['k_norm'][0])
    vc, _ = compress_branch(vc_raw, lp, 1)
    ks_blk, vs_blk = to_blocks(ks), to_blocks(vs)
    pad = ((0, 0), (WINDOW, 0), (0, 0), (0, 0))
    kw_pad, vw_pad = jnp.pad(kw, pad), jnp.pad(vw, pad)
    nq = T // Q_BLOCK
    qb = jnp.moveaxis(q.reshape(B, nq, Q_BLOCK, N_KV, GROUP, HEAD_DIM), 1, 0)
    gb = jnp.moveaxis(gates.reshape(B, nq, Q_BLOCK, N_KV, GROUP, 3), 1, 0)

    def one_block(args):
        i, q_i, g_i = args
        start = i * Q_BLOCK
        t_pos = start + jnp.arange(Q_BLOCK, dtype=jnp.int32)
        kw_i = lax.dynamic_slice_in_dim(kw_pad, start, WINDOW + Q_BLOCK, axis=1)
        vw_i = lax.dynamic_slice_in_dim(vw_pad, start, WINDOW + Q_BLOCK, axis=1)
        w_pos = start - WINDOW + jnp.arange(WINDOW + Q_BLOCK, dtype=jnp.int32)
        return nsa_block(q_i, t_pos, g_i, kc, vc, kc_end, ks_blk, vs_blk, kw_i, vw_i, w_pos, rel_bias)

    o = lax.map(one_block, (jnp.arange(nq, dtype=jnp.int32), qb, gb))
    o = jnp.moveaxis(o, 0, 1).reshape(B, T, ATTN_WIDTH)
    new_win = jnp.stack([kw, vw], axis=2)[:, T - min(WINDOW, T):]
    return o, (jnp.stack([kc_raw, vc_raw], axis=2), jnp.stack([ks, vs], axis=2), new_win)

def nsa_sample(q, gates, kc_raw, vc_raw, ks, vs, kw, vw, cache_cmp, cache_sel, cache_win, page_table, lp, rel_bias):
    Bd, Tn = q.shape[0], q.shape[1]
    past = page_table.shape[1] * cache_cmp.shape[1]
    t_pos = past + jnp.arange(Tn, dtype=jnp.int32)
    past_cmp = cache_cmp[page_table].reshape(Bd, past, 2, N_KV, HEAD_DIM)
    past_sel = cache_sel[page_table].reshape(Bd, past, 2, N_KV, HEAD_DIM)
    kc, kc_end = compress_branch(jnp.concatenate([past_cmp[:, :, 0], kc_raw], axis=1), lp, 0)
    kc = rms_norm(kc, lp['k_norm'][0])
    vc, _ = compress_branch(jnp.concatenate([past_cmp[:, :, 1], vc_raw], axis=1), lp, 1)
    ks_blk = to_blocks(jnp.concatenate([past_sel[:, :, 0], ks], axis=1))
    vs_blk = to_blocks(jnp.concatenate([past_sel[:, :, 1], vs], axis=1))
    wk = cache_win.shape[1]
    win = jnp.concatenate([cache_win, jnp.stack([kw, vw], axis=2)], axis=1)
    w_pos = past - wk + jnp.arange(wk + Tn, dtype=jnp.int32)
    o = nsa_block(q, t_pos, gates, kc, vc, kc_end, ks_blk, vs_blk, win[:, :, 0], win[:, :, 1], w_pos, rel_bias)
    new_win = win[:, wk + Tn - min(WINDOW, wk + Tn):]
    return o.reshape(Bd, Tn, ATTN_WIDTH), (jnp.stack([kc_raw, vc_raw], axis=2), jnp.stack([ks, vs], axis=2), new_win)

def conformer_conv(glu_in, hist, lp):
    u = glu_in[..., :CONV_WIDTH] * jax.nn.sigmoid(glu_in[..., CONV_WIDTH:])
    uh = jnp.concatenate([hist.astype(u.dtype), u], axis=1)
    y = lax.conv_general_dilated(uh, lp['conv_w'][:, None, :], window_strides=(1,), padding='VALID',
                                 dimension_numbers=('NWC', 'WIO', 'NWC'), feature_group_count=CONV_WIDTH)
    y = jax.nn.silu(layer_norm(y + lp['conv_b'], lp['conv_ln_g'], lp['conv_ln_b']))
    return y, uh[:, uh.shape[1] - (CONV_K - 1):]

def peer(h, lp):
    shp = h.shape
    xt = h.reshape(-1, D_MODEL)
    n = xt.shape[0]
    nb = -(-n // PEER_BLOCK)
    xt = jnp.pad(xt, ((0, nb * PEER_BLOCK - n), (0, 0))).reshape(nb, PEER_BLOCK, D_MODEL)
    q_w, sub_keys, eu, ev = lp['peer_q'], lp['peer_keys'], lp['expert_u'], lp['expert_v']

    def one_block(xb):
        q = (xb @ q_w).reshape(PEER_BLOCK, PEER_HEADS, 2, PEER_DQ // 2)
        s = jnp.einsum('thcd,hcnd->thcn', q, sub_keys).astype(jnp.float32)
        s1, i1 = lax.top_k(s[:, :, 0], PEER_TOPK)
        s2, i2 = lax.top_k(s[:, :, 1], PEER_TOPK)
        cand = (s1[..., :, None] + s2[..., None, :]).reshape(PEER_BLOCK, PEER_HEADS, PEER_TOPK * PEER_TOPK)
        cidx = (i1[..., :, None] * N_KEYS + i2[..., None, :]).reshape(PEER_BLOCK, PEER_HEADS, PEER_TOPK * PEER_TOPK)
        top_s, pos = lax.top_k(cand, PEER_TOPK)
        eidx = jnp.take_along_axis(cidx, pos, axis=-1)
        g = jax.nn.softmax(top_s, axis=-1)
        u = eu[eidx]
        v = ev[eidx]
        a = jax.nn.gelu(jnp.einsum('td,thkd->thk', xb, u).astype(jnp.float32))
        return jnp.einsum('thk,thkd->td', (g * a).astype(v.dtype), v)

    y = lax.map(one_block, xt).reshape(-1, D_MODEL)[:n]
    return y.reshape(shp)

def split_points():
    pts, acc = [], 0
    for s in SPLIT_SIZES[:-1]:
        acc += s
        pts.append(acc)
    return pts

def layer(x, c, conv_hist, lp, rel_bias, cache):
    B, T = x.shape[0], x.shape[1]
    mod = (jax.nn.silu(c) @ lp['w_ada'] + lp['b_ada'])[:, None, :]
    sh1, sc1, gt1, sh2, sc2, gt2 = jnp.split(mod, 6, axis=-1)
    h = rms_norm(x, lp['norm1']) * (1 + sc1) + sh1
    zq, zkc, zvc, zks, zvs, zkw, zvw, zg, zglu = jnp.split(h @ lp['w_in'], split_points(), axis=-1)

    def kv(z):
        return z.reshape(B, T, N_KV, HEAD_DIM)

    q = rms_norm(zq.reshape(B, T, N_KV, GROUP, HEAD_DIM), lp['q_norm'])
    ks = rms_norm(kv(zks), lp['k_norm'][1])
    kw = rms_norm(kv(zkw), lp['k_norm'][2])
    gates = jax.nn.sigmoid(zg.reshape(B, T, N_KV, GROUP, 3))
    if cache is None:
        o_attn, attn_state = nsa_prompt(q, gates, kv(zkc), kv(zvc), ks, kv(zvs), kw, kv(zvw), lp, rel_bias)
    else:
        cache_cmp, cache_sel, cache_win, page_table = cache
        o_attn, attn_state = nsa_sample(q, gates, kv(zkc), kv(zvc), ks, kv(zvs), kw, kv(zvw),
                                        cache_cmp, cache_sel, cache_win, page_table, lp, rel_bias)
    o_conv, conv_state = conformer_conv(zglu, conv_hist, lp)
    mix = jnp.concatenate([rms_norm(o_attn, lp['attn_out_norm']), o_conv * lp['conv_out_scale']], axis=-1) @ lp['w_out']
    x = x + gt1 * mix
    h2 = rms_norm(x, lp['norm2']) * (1 + sc2) + sh2
    x = x + gt2 * peer(h2, lp)
    return x, attn_state, conv_state

def setup_inputs(seed: int = 0) -> dict:
    key = jax.random.key(seed)
    k = jax.random.split(key, 36)
    n_pages = PAST_LEN // PAGE_SIZE
    n_used = DEC_BATCH * n_pages
    n_pool = n_used + max(1, n_used // 4)
    win_keep = min(WINDOW, PAST_LEN)
    f32 = jnp.float32

    def nrm(kk, shape, s):
        return jax.random.normal(kk, shape, f32) * s

    def gain(kk, shape):
        return 1.0 + 0.02 * jax.random.normal(kk, shape, f32)

    page_table = jax.random.permutation(k[8], n_pool)[:n_used].reshape(DEC_BATCH, n_pages).astype(jnp.int32)
    return {
        'x_prompt': nrm(k[0], (BATCH, SEQ, D_MODEL), 1.0),
        'x_sample': nrm(k[1], (DEC_BATCH, DEC_SEQ, D_MODEL), 1.0),
        'c_prompt': nrm(k[2], (BATCH, D_MODEL), 1.0),
        'c_sample': nrm(k[3], (DEC_BATCH, D_MODEL), 1.0),
        'cache_cmp_kv': nrm(k[4], (DEPTH, n_pool, PAGE_SIZE, 2, N_KV, HEAD_DIM), 1.0),
        'cache_sel_kv': nrm(k[5], (DEPTH, n_pool, PAGE_SIZE, 2, N_KV, HEAD_DIM), 1.0),
        'cache_win_kv': nrm(k[6], (DEPTH, DEC_BATCH, win_keep, 2, N_KV, HEAD_DIM), 1.0),
        'state_conv': nrm(k[7], (DEPTH, DEC_BATCH, CONV_K - 1, CONV_WIDTH), 0.5),
        'page_table': page_table,
        'rel_bias': nrm(k[9], (N_BUCKETS, N_HEADS), 0.5),
        'w_ada': nrm(k[10], (DEPTH, D_MODEL, 6 * D_MODEL), 0.5 * D_MODEL ** -0.5),
        'b_ada': nrm(k[11], (DEPTH, 6 * D_MODEL), 0.02),
        'norm1': gain(k[12], (DEPTH, D_MODEL)),
        'w_in': nrm(k[13], (DEPTH, D_MODEL, IN_COLS), D_MODEL ** -0.5),
        'q_norm': gain(k[14], (DEPTH, HEAD_DIM)),
        'k_norm': gain(k[15], (DEPTH, 3, HEAD_DIM)),
        'cmp_pe': nrm(k[16], (DEPTH, 2, CMP_LEN, HEAD_DIM), 0.1),
        'cmp_w1': nrm(k[17], (DEPTH, 2, CMP_LEN * HEAD_DIM, CMP_HIDDEN), (CMP_LEN * HEAD_DIM) ** -0.5),
        'cmp_b1': nrm(k[18], (DEPTH, 2, CMP_HIDDEN), 0.02),
        'cmp_w2': nrm(k[19], (DEPTH, 2, CMP_HIDDEN, HEAD_DIM), CMP_HIDDEN ** -0.5),
        'cmp_b2': nrm(k[20], (DEPTH, 2, HEAD_DIM), 0.02),
        'conv_w': nrm(k[21], (DEPTH, CONV_K, CONV_WIDTH), CONV_K ** -0.5),
        'conv_b': nrm(k[22], (DEPTH, CONV_WIDTH), 0.02),
        'conv_ln_g': gain(k[23], (DEPTH, CONV_WIDTH)),
        'conv_ln_b': nrm(k[24], (DEPTH, CONV_WIDTH), 0.02),
        'attn_out_norm': gain(k[25], (DEPTH, ATTN_WIDTH)),
        'conv_out_scale': gain(k[26], (DEPTH, CONV_WIDTH)),
        'w_out': nrm(k[27], (DEPTH, D_MODEL, D_MODEL), D_MODEL ** -0.5),
        'norm2': gain(k[28], (DEPTH, D_MODEL)),
        'peer_q': nrm(k[29], (DEPTH, D_MODEL, PEER_HEADS * PEER_DQ), D_MODEL ** -0.5),
        'peer_keys': nrm(k[30], (DEPTH, PEER_HEADS, 2, N_KEYS, PEER_DQ // 2), (PEER_DQ // 2) ** -0.5),
        'expert_u': nrm(k[31], (DEPTH, N_EXPERTS, D_MODEL), D_MODEL ** -0.5),
        'expert_v': nrm(k[32], (DEPTH, N_EXPERTS, D_MODEL), 1.0),
    }

def reference(x_prompt, x_sample, c_prompt, c_sample, cache_cmp_kv, cache_sel_kv, cache_win_kv, state_conv,
              page_table, rel_bias, w_ada, b_ada, norm1, w_in, q_norm, k_norm, cmp_pe, cmp_w1, cmp_b1, cmp_w2,
              cmp_b2, conv_w, conv_b, conv_ln_g, conv_ln_b, attn_out_norm, conv_out_scale, w_out, norm2,
              peer_q, peer_keys, expert_u, expert_v):
    y_prompt, y_sample = x_prompt, x_sample
    p_cmp, p_sel, p_win, p_conv = [], [], [], []
    s_cmp, s_sel, s_win, s_conv = [], [], [], []
    for l in range(DEPTH):
        lp = {
            'w_ada': w_ada[l], 'b_ada': b_ada[l], 'norm1': norm1[l], 'w_in': w_in[l],
            'q_norm': q_norm[l], 'k_norm': k_norm[l], 'cmp_pe': cmp_pe[l], 'cmp_w1': cmp_w1[l],
            'cmp_b1': cmp_b1[l], 'cmp_w2': cmp_w2[l], 'cmp_b2': cmp_b2[l], 'conv_w': conv_w[l],
            'conv_b': conv_b[l], 'conv_ln_g': conv_ln_g[l], 'conv_ln_b': conv_ln_b[l],
            'attn_out_norm': attn_out_norm[l], 'conv_out_scale': conv_out_scale[l], 'w_out': w_out[l],
            'norm2': norm2[l], 'peer_q': peer_q[l], 'peer_keys': peer_keys[l],
            'expert_u': expert_u[l], 'expert_v': expert_v[l],
        }
        hist0 = jnp.zeros((y_prompt.shape[0], CONV_K - 1, CONV_WIDTH), y_prompt.dtype)
        y_prompt, (a_c, a_s, a_w), cv = layer(y_prompt, c_prompt, hist0, lp, rel_bias, None)
        p_cmp.append(a_c)
        p_sel.append(a_s)
        p_win.append(a_w)
        p_conv.append(cv)
        y_sample, (b_c, b_s, b_w), cvs = layer(y_sample, c_sample, state_conv[l], lp, rel_bias,
                                               (cache_cmp_kv[l], cache_sel_kv[l], cache_win_kv[l], page_table))
        s_cmp.append(b_c)
        s_sel.append(b_s)
        s_win.append(b_w)
        s_conv.append(cvs)
    new_cmp_prompt = jnp.stack(p_cmp)
    new_sel_prompt = jnp.stack(p_sel)
    new_win_prompt = jnp.stack(p_win)
    new_conv_prompt = jnp.stack(p_conv)
    new_cmp_sample = jnp.stack(s_cmp)
    new_sel_sample = jnp.stack(s_sel)
    new_win_sample = jnp.stack(s_win)
    new_conv_sample = jnp.stack(s_conv)
    return (y_prompt, y_sample, new_cmp_prompt, new_sel_prompt, new_win_prompt, new_conv_prompt,
            new_cmp_sample, new_sel_sample, new_win_sample, new_conv_sample)


_drawn_inputs = setup_inputs


def setup_inputs(seed=0):
    import zlib

    import numpy as np

    out = dict(_drawn_inputs(seed))
    spreads = {}
    factors = {'norm1': 2.791,
     'q_norm': 22.322,
     'k_norm': 13.008,
     'cmp_b1': 31.014,
     'conv_b': 4.577,
     'conv_ln_g': 42.917,
     'conv_ln_b': 42.804,
     'attn_out_norm': 200.0,
     'conv_out_scale': 42.355,
     'rel_bias': 13.435,
     'cmp_pe': 3.96,
     'cmp_b2': 27.905,
     'norm2': 52.431}
    for name, (base, spread) in spreads.items():
        noise = np.random.default_rng([zlib.crc32(name.encode()), seed]).standard_normal(out[name].shape)
        drawn = base * np.exp(spread * noise) if base else spread * noise
        out[name] = jnp.asarray(drawn.astype(out[name].dtype))
    for name, factor in factors.items():
        out[name] = (out[name] * factor).astype(out[name].dtype)
    return out
```

```python
from contextlib import ExitStack

import numpy as np

import concourse.bass as bass
from concourse import mybir

ALU = mybir.AluOpType
ACT = mybir.ActivationFunctionType
AX = mybir.AxisListType.X
F32 = mybir.dt.float32
I32 = mybir.dt.int32
U32 = mybir.dt.uint32

P = 128
D = 1024
KD = D // P
SEQ = 512
NB = 8
DT = 4
NS = NB * DT
PAST = 1024
PAGE = 128
PAGES = PAST // PAGE
HD = 64
H = 8
G = 2
R = H // G
AW = H * HD
CW = D - AW
CK = 31
CMP_HID = 256
WIN = 512
EPS = 1e-6
TILES = 5
PT = SEQ // P
TOK = SEQ + NS
ROWCOLS = AW + 6 * P + 3 * H
INCOLS = ROWCOLS + 2 * CW
KC, VC, KS, VS, KW, VW = (AW + P * i for i in range(6))
NC_P = SEQ // 16 - 1
NC_S = PAST // 16 - 1
NSEL = (PAST + DT + 63) // 64
PH = 8
NK = 128
TK = 16
NEG = -1.0e30
DMAX = 1027
OHW = DMAX + P + 1
TW = 640
BUCKETS = 32
SEQW = CK - 1 + SEQ
SMPW = CK - 1 + DT
CONVW = SEQW + NB * SMPW
CONVO = CONVW - (CK - 1)


def rows(i):
    return P if i < PT else NS


def span(ap, axis, n):
    out = ap.unsqueeze(axis)
    shape = list(out.shape)
    shape[axis] = n
    return out.to_broadcast(shape)


class Chain:

    def __init__(self, eng, sem):
        self.eng, self.sem, self.n = eng, sem, 0

    def __call__(self, ins):
        self.n += 1
        ins.then_inc(self.sem, 1)
        self.eng.wait_ge(self.sem, self.n)


def shape_constants():
    part = np.arange(P)
    ident = np.eye(P, dtype=np.float32)
    b4, g, t = part // 32, part // 16 % 2, part % 4
    same = (b4[:, None] == b4) & (g[:, None] == g) & (t[:, None] == t)
    other = np.zeros((P, 2, NB), np.float32)
    for hi in range(2):
        other[:, hi] = np.where(np.arange(NB)[None] == (b4 + 4 * hi)[:, None], 0.0, NEG)
    iota = np.tile(np.arange(32, dtype=np.float32), (P, 1))
    pick = np.zeros((P, P + NS), np.float32)
    pick[0, :P] = 1.0
    for tok in range(NS):
        pick[1 + tok // DT, P + tok] = 1.0
    consts = np.concatenate([ident, same.astype(np.float32), other.reshape(P, -1), iota, pick], axis=1)
    dist = DMAX - np.arange(OHW)
    n = np.maximum(dist, 0)
    nf = np.maximum(n, 1).astype(np.float32)
    large = 16 + (np.log(nf / np.float32(16)) / np.float32(np.log(8.0)) * 16).astype(np.int32)
    bucket = np.where(n < 16, n, np.minimum(large, BUCKETS - 1))
    onehot = np.zeros((BUCKETS + 2, OHW), np.float32)
    onehot[bucket[dist >= 0], np.nonzero(dist >= 0)[0]] = 1.0
    onehot[BUCKETS] = dist < 0
    onehot[BUCKETS + 1] = dist >= WIN
    return consts, onehot


C_ID, C_SAME, C_OTHER, C_IOTA, C_PICK = 0, 128, 256, 272, 304
C_W = C_PICK + P + NS


class Env:

    def __init__(self, nc, ctx, io):
        self.nc, self.ctx, self.sems = nc, ctx, []
        self.x_prompt = io["x_prompt"]
        self.x_sample = io["x_sample"]
        self.c_prompt = io["c_prompt"]
        self.c_sample = io["c_sample"]
        self.cache_cmp_kv = io["cache_cmp_kv"]
        self.cache_sel_kv = io["cache_sel_kv"]
        self.cache_win_kv = io["cache_win_kv"]
        self.state_conv = io["state_conv"]
        self.page_table = io["page_table"]
        self.rel_bias = io["rel_bias"]
        self.w_ada = io["w_ada"]
        self.b_ada = io["b_ada"]
        self.norm1 = io["norm1"]
        self.w_in = io["w_in"]
        self.q_norm = io["q_norm"]
        self.k_norm = io["k_norm"]
        self.cmp_pe = io["cmp_pe"]
        self.cmp_w1 = io["cmp_w1"]
        self.cmp_b1 = io["cmp_b1"]
        self.cmp_w2 = io["cmp_w2"]
        self.cmp_b2 = io["cmp_b2"]
        self.conv_w = io["conv_w"]
        self.conv_b = io["conv_b"]
        self.conv_ln_g = io["conv_ln_g"]
        self.conv_ln_b = io["conv_ln_b"]
        self.attn_out_norm = io["attn_out_norm"]
        self.conv_out_scale = io["conv_out_scale"]
        self.w_out = io["w_out"]
        self.norm2 = io["norm2"]
        self.peer_q = io["peer_q"]
        self.peer_keys = io["peer_keys"]
        self.expert_u = io["expert_u"]
        self.expert_v = io["expert_v"]
        self.consts_in = io["consts_in"]
        self.onehot_in = io["onehot_in"]
        self.y_prompt = io["y_prompt"]
        self.y_sample = io["y_sample"]
        self.new_cmp_prompt = io["new_cmp_prompt"]
        self.new_sel_prompt = io["new_sel_prompt"]
        self.new_win_prompt = io["new_win_prompt"]
        self.new_conv_prompt = io["new_conv_prompt"]
        self.new_cmp_sample = io["new_cmp_sample"]
        self.new_sel_sample = io["new_sel_sample"]
        self.new_win_sample = io["new_win_sample"]
        self.new_conv_sample = io["new_conv_sample"]

    def sem(self, name):
        handle = self.nc.alloc_semaphore(name=name)
        self.sems.append(handle)
        return handle

    def free_sems(self):
        self.nc.clear_and_free_semaphores(self.sems)
        self.nc.all_engine_barrier()
        self.sems = []

    def sb(self, name, shape, dt=F32, ctx=None):
        return (ctx or self.ctx).enter_context(self.nc.sbuf_tensor(name, shape, dt))


def keep(e):
    nc = e.nc
    e.bank = [e.ctx.enter_context(nc.psum_tensor(f"bank{i}", [P, 512], F32)) for i in range(8)]
    e.consts = e.sb("consts_sb", [P, C_W])
    e.ident = e.consts[:, C_ID:C_ID + P]
    e.skew = nc.dram_tensor("skew_dram", [H, P * TW], F32, kind="Internal").ap()
    e.gate_dram = nc.dram_tensor("gate_dram", [NS, 3 * H], F32, kind="Internal").ap()
    e.s_store = nc.alloc_semaphore(name="results_stored")
    e.stores = 0


def stage_ada(e):
    nc = e.nc
    with ExitStack() as ctx:
        NW = 12
        craw = e.sb("craw", [9, D], ctx=ctx)
        cexp = e.sb("cexp", [9, D], ctx=ctx)
        cT = e.sb("cT", [P, KD, 9], ctx=ctx)
        bada = e.sb("b_ada_ring", [9, 3, 512], ctx=ctx)
        mod = e.sb("mod_ring", [9, 3, 512], ctx=ctx)
        norms = e.sb("norms", [P, 2, D], ctx=ctx)
        w = e.sb("w_ada_ring", [P, 3, KD, 512], ctx=ctx)
        onehot = e.sb("onehot_sb", [BUCKETS + 2, OHW], ctx=ctx)
        tbl = e.sb("tbl", [BUCKETS + 2, H], ctx=ctx)
        trow = e.sb("trow", [BUCKETS + 2, DT, 4, H, DT], ctx=ctx)
        tcol = e.sb("tcol", [BUCKETS + 1, H, P], ctx=ctx)
        skw = e.sb("skw", [P, TW], ctx=ctx)

        s_in = e.sem("ada_inputs")
        s_rel = e.sem("rel_bias_loaded")
        s_w = [e.sem(f"w_ada_loaded{i}") for i in range(3)]
        s_tbl0 = e.sem("table_filled")
        s_ce = e.sem("c_exp")
        s_c = e.sem("c_silu")
        s_cT = e.sem("c_transposed")
        s_cTs = e.sem("c_transposed_kept")
        s_ch = e.sem("ada_vector_chain")
        s_mm = e.sem("mod_product")
        s_mod = e.sem("mod_kept")
        s_sp = e.sem("mod_spread")
        s_spk = e.sem("mod_spread_kept")
        s_trow = e.sem("bias_rows_ready")
        s_bp = e.sem("bias_product")
        s_bk = e.sem("bias_kept")
        s_skw = e.sem("skew_written")
        s_skr = e.sem("skew_read")

        w_ada = e.w_ada.rearrange("o (k p) n -> p (o k) n", p=P)
        NBIAS = 2 * H + 4

        with nc.Block() as block:
            @block.sync
            def _(sp):
                sp.dma_start(e.consts[:], e.consts_in).then_inc(s_in, 16)
                sp.dma_start(craw[0:1, :], e.c_prompt).then_inc(s_in, 16)
                sp.dma_start(craw[1:9, :], e.c_sample).then_inc(s_in, 16)
                sp.dma_start(norms[:, 0, :], e.norm1.to_broadcast([P, D])).then_inc(s_in, 16)
                sp.dma_start(norms[:, 1, :], e.norm2.to_broadcast([P, D])).then_inc(s_in, 16)
                sp.dma_start(onehot[:], e.onehot_in).then_inc(s_rel, 16)
                sp.wait_ge(s_tbl0, 1)
                sp.dma_start(tbl[0:BUCKETS, :], e.rel_bias).then_inc(s_rel, 16)
                for n in range(NW):
                    if n >= 3:
                        sp.wait_ge(s_mm, n - 2)
                    sp.dma_start(w[:, n % 3], w_ada[:, :, n * 512:(n + 1) * 512]).then_inc(s_w[n % 3], 16)
                    if n >= 3:
                        sp.wait_ge(s_mod, n - 2)
                    sp.dma_start(bada[:, n % 3], e.b_ada[:, n * 512:(n + 1) * 512].to_broadcast([9, 512])
                                 ).then_inc(s_w[n % 3], 16)

            @block.gpsimd
            def _(pool):
                for h in range(H):
                    pool.wait_ge(s_bk, 2 * h + 2)
                    pool.dma_start(e.skew[h].rearrange("(p c) -> p c", p=P), skw[:]).then_inc(s_skw, 16)
                    pool.wait_ge(s_skw, 16 * (h + 1))
                    src = bass.AP(e.skew.tensor, h * P * TW + P - 1, [[TW - 1, P], [1, 512]])
                    pool.dma_start(e.bias_p[:, h, :], src).then_inc(s_skr, 16)
                pool.wait_ge(s_skr, 16 * H)

            @block.scalar
            def _(act):
                act.wait_ge(s_in, 80)
                nc.scalar.activation(cexp[:], craw[:], ACT.Exp, scale=-1.0).then_inc(s_ce, 1)

            @block.tensor
            def _(pe):
                pe.wait_ge(s_c, 1)
                for k in range(KD):
                    last = nc.tensor.transpose(e.bank[0][:, k * 9:(k + 1) * 9], craw[:, k * P:(k + 1) * P],
                                               e.ident[0:9, 0:9])
                last.then_inc(s_cT, 1)
                pe.wait_ge(s_cTs, 1)

                def spread(n):
                    pe.wait_ge(s_mod, n + 1)
                    for s in range(2):
                        j = 2 * n + s
                        if j >= 2:
                            pe.wait_ge(s_spk, j - 1)
                        r = P if s == 0 else NS
                        nc.tensor.matmul(e.bank[2 + j % 2][0:r, :], e.consts[0:9, C_PICK + s * P:C_PICK + s * P + r],
                                         mod[:, n % 3], start=True, stop=True).then_inc(s_sp, 1)

                for n in range(NW):
                    pe.wait_ge(s_w[n % 3], 32 * (n // 3 + 1))
                    if n >= 2:
                        pe.wait_ge(s_mod, n - 1)
                    for k in range(KD):
                        last = nc.tensor.matmul(e.bank[n % 2][0:9, :], cT[:, k, :], w[:, n % 3, k, :],
                                                start=(k == 0), stop=(k == KD - 1))
                    last.then_inc(s_mm, 1)
                    if n >= 1:
                        spread(n - 1)
                spread(NW - 1)
                pe.wait_ge(s_trow, 1)
                for h in range(H):
                    for half in range(2):
                        j = 2 * h + half
                        if j >= 2:
                            pe.wait_ge(s_bk, j - 1)
                        nc.tensor.matmul(e.bank[4 + j % 2][:, 0:TW // 2], tcol[:, h, :],
                                         onehot[0:BUCKETS + 1, DMAX - 511 + half * 320:DMAX - 511 + half * 320 + 320],
                                         start=True, stop=True).then_inc(s_bp, 1)
                for q, (kk, pos, n) in enumerate([(BUCKETS + 1, 0, 512), (BUCKETS + 1, 512, 512),
                                                  (BUCKETS + 1, PAST, DT), (BUCKETS + 2, PAST - WIN, 512)]):
                    j = 2 * H + q
                    pe.wait_ge(s_bk, j - 1)
                    for t in range(DT):
                        c = DT - 1 - t + pos
                        last = nc.tensor.matmul(e.bank[4 + j % 2][:, 0:n],
                                                trow[0:kk, t].rearrange("k b h t -> k (b h t)"),
                                                onehot[0:kk, c:c + n], start=(t == 0), stop=(t == DT - 1))
                    last.then_inc(s_bp, 1)

            @block.vector
            def _(dve):
                link = Chain(dve, s_ch)
                nc.vector.memset(tbl[:], NEG).then_inc(s_tbl0, 1)
                link(nc.vector.memset(trow[:], 0.0))
                dve.wait_ge(s_ce, 1)
                link(nc.vector.tensor_scalar_add(cexp[:], cexp[:], 1.0))
                link(nc.vector.reciprocal(cexp[:], cexp[:]))
                nc.vector.tensor_tensor(craw[:], craw[:], cexp[:], ALU.mult).then_inc(s_c, 1)
                dve.wait_ge(s_cT, 1)
                nc.vector.tensor_copy(cT[:].rearrange("p k c -> p (k c)"), e.bank[0][:, 0:KD * 9]).then_inc(s_cTs, 1)
                dve.wait_ge(s_rel, 32)
                nc.vector.tensor_copy(tcol[:], span(tbl[0:BUCKETS + 1, :], 2, P))
                for t in range(DT):
                    last = nc.vector.tensor_copy(trow[:, t, :, :, t], span(tbl[:], 1, 4))
                last.then_inc(s_trow, 1)

                def keep_spread(n):
                    m, half = n // 2, n % 2
                    for s in range(2):
                        r = P if s == 0 else NS
                        dve.wait_ge(s_sp, 2 * n + s + 1)
                        src = e.bank[2 + (2 * n + s) % 2][0:r, :]
                        kept = e.mods1[0:r, s, m] if m < 2 else e.mods[0:r, s, m - 2]
                        dst = kept[:, half * 512:(half + 1) * 512]
                        if m in (1, 4):
                            ins = nc.vector.scalar_tensor_tensor(dst, src, 1.0,
                                                                 norms[0:r, m // 4, half * 512:(half + 1) * 512],
                                                                 ALU.add, ALU.mult)
                        else:
                            ins = nc.vector.tensor_copy(dst, src)
                        ins.then_inc(s_spk, 1)

                for n in range(NW):
                    dve.wait_ge(s_mm, n + 1)
                    nc.vector.tensor_tensor(mod[:, n % 3], e.bank[n % 2][0:9, :],
                                            bada[:, n % 3], ALU.add).then_inc(s_mod, 1)
                    if n >= 1:
                        keep_spread(n - 1)
                keep_spread(NW - 1)
                for h in range(H):
                    for half in range(2):
                        j = 2 * h + half
                        dve.wait_ge(s_bp, j + 1)
                        if h >= 1 and half == 0:
                            dve.wait_ge(s_skw, 16 * h)
                        nc.vector.tensor_copy(skw[:, half * 320:(half + 1) * 320],
                                              e.bank[4 + j % 2][:, 0:320]).then_inc(s_bk, 1)
                for q, dst in enumerate([e.bias_s[:, 0:512], e.bias_s[:, 512:PAST], e.bias_n4[:], e.bias_w[:]]):
                    j = 2 * H + q
                    dve.wait_ge(s_bp, j + 1)
                    nc.vector.tensor_copy(dst, e.bank[4 + j % 2][:, 0:dst.shape[1]]).then_inc(s_bk, 1)
                dve.wait_ge(s_bk, NBIAS)
                other = e.consts[:, C_OTHER:C_OTHER + 2 * NB].rearrange("p (a b) -> p a b", a=2)
                for hi in range(2):
                    nc.vector.tensor_tensor(e.bias_new[:, hi], span(e.bias_n4[:], 1, NB), span(other[:, hi], 2, DT),
                                            ALU.add).then_inc(s_bk, 1)
                dve.wait_ge(s_bk, NBIAS + 2)

def stage_project(e):
    nc = e.nc
    with ExitStack() as ctx:
        hT = e.sb("hT", [P, KD, TOK], ctx=ctx)
        xt = e.sb("x_tiles", [P, 2, D], ctx=ctx)
        ht = e.sb("h_tiles", [P, 2, D], ctx=ctx)
        ss = e.sb("x_square_sums", [P, TILES], ctx=ctx)
        rs = e.sb("x_rstd", [P, TILES], ctx=ctx)
        w = e.sb("w_in_ring", [P, 2, KD, 512], ctx=ctx)
        eb = e.sb("glu_exp", [P, 2, TOK], ctx=ctx)
        hist = e.sb("conv_history", [120, 2, CW], ctx=ctx)
        cwr = e.sb("conv_weight_rows", [CK + 1, CW], ctx=ctx)
        usn = e.sb("new_conv_columns", [P, 4, NS], ctx=ctx)
        urow = e.sb("new_conv_rows", [NS, 2, CW], ctx=ctx)

        s_x = [e.sem(f"x_loaded{i}") for i in range(2)]
        s_w = [e.sem(f"w_in_loaded{i}") for i in range(2)]
        s_cv = e.sem("conv_inputs_loaded")
        s_sq = e.sem("x_squared")
        s_hc = e.sem("h_chain")
        s_h = e.sem("h_rows")
        s_var = e.sem("x_variance")
        s_rs = e.sem("x_rstd_ready")
        s_hT = e.sem("h_transposed")
        s_hk = e.sem("h_transposed_kept")
        s_z = e.sem("z_product")
        s_zk = e.sem("z_kept")
        s_g = e.sem("glu_product")
        s_gk = e.sem("glu_kept")
        s_ge = e.sem("glu_exp_ready")
        s_gu = e.sem("glu_done")
        s_cT = e.sem("conv_transposed")
        s_cK = e.sem("conv_transposed_kept")
        s_un = e.sem("new_conv_compact")
        s_ut = e.sem("new_conv_transposed")
        s_uk = e.sem("new_conv_rows_kept")

        w_in = e.w_in.rearrange("o (k p) n -> p (o k) n", p=P)
        chunks = [(0, 512), (512, 512), (1024, ROWCOLS - 1024), (ROWCOLS, CW), (ROWCOLS + CW, CW)]
        x_of = [e.x_prompt[0, i * P:(i + 1) * P, :] for i in range(PT)] + [e.x_sample.rearrange("b t d -> (b t) d")]
        conv_s = e.convu[:, :, SEQW:].rearrange("p c (b w) -> p c b w", b=NB)

        with nc.Block() as block:
            @block.sync
            def _(sp):
                for i in range(2):
                    sp.dma_start(xt[0:rows(i), i], x_of[i]).then_inc(s_x[i], 16)
                for c in range(2):
                    sp.dma_start(w[:, c, :, 0:chunks[c][1]],
                                 w_in[:, :, chunks[c][0]:chunks[c][0] + chunks[c][1]]).then_inc(s_w[c], 16)
                sp.dma_start(cwr[0:CK, :], e.conv_w[0]).then_inc(s_cv, 16)
                sp.dma_start(cwr[CK:CK + 1, :], e.conv_b).then_inc(s_cv, 16)
                st = e.state_conv.rearrange("o (a b) w c -> (o a) (b w) c", a=2)
                for a in range(2):
                    sp.dma_start(hist[:, a], st[a]).then_inc(s_cv, 16)
                for i in range(2, TILES):
                    sp.wait_ge(s_h, i - 1)
                    sp.dma_start(xt[0:rows(i), i % 2], x_of[i]).then_inc(s_x[i % 2], 16)
                for c in range(2, 5):
                    if c - 2 < 3:
                        sp.wait_ge(s_z, 5 * (c - 1))
                    sp.dma_start(w[:, c % 2, :, 0:chunks[c][1]],
                                 w_in[:, :, chunks[c][0]:chunks[c][0] + chunks[c][1]]).then_inc(s_w[c % 2], 16)
                sp.dma_start(e.new_conv_sample[0, :, 0:CK - 1 - DT, :],
                             e.state_conv[0, :, DT:, :]).then_inc(e.s_store, 16)
                sp.wait_ge(s_uk, 1)
                sp.dma_start(e.new_conv_prompt[0, 0], urow[0:CK - 1, 0]).then_inc(e.s_store, 16)
                sp.wait_ge(s_uk, 2)
                for b in range(NB):
                    sp.dma_start(e.new_conv_sample[0, b, CK - 1 - DT:, :],
                                 urow[b * DT:(b + 1) * DT, 1]).then_inc(e.s_store, 16)
                e.stores += 2 + NB
                sp.wait_ge(e.s_store, 16 * e.stores)

            def keep_hT(act, i):
                act.wait_ge(s_hT, i + 1)
                r = rows(i)
                for q in range(2):
                    ins = nc.scalar.copy(hT[:, 4 * q:4 * q + 4, i * P:i * P + r],
                                         e.bank[2 * (i % 2) + q][:, 0:4 * r].rearrange("p (k n) -> p k n", k=4))
                ins.then_inc(s_hk, 1)

            @block.scalar
            def _(act):
                for i in range(TILES):
                    act.wait_ge(s_x[i % 2], 16 * (i // 2 + 1))
                    if i >= 2:
                        act.wait_ge(s_h, i - 1)
                        act.wait_ge(s_hT, i - 1)
                    r = rows(i)
                    nc.scalar.activation(ht[0:r, i % 2], xt[0:r, i % 2], ACT.Square,
                                         accum_out=ss[0:r, i:i + 1]).then_inc(s_sq, 1)
                    act.wait_ge(s_var, i + 1)
                    nc.scalar.activation(rs[0:r, i:i + 1], rs[0:r, i:i + 1], ACT.Sqrt).then_inc(s_rs, 1)
                    if i >= 1:
                        keep_hT(act, i - 1)
                keep_hT(act, TILES - 1)
                for c in range(3):
                    for i in range(TILES):
                        j = 5 * c + i
                        act.wait_ge(s_z, j + 1)
                        r, n = rows(i), chunks[c][1]
                        nc.scalar.copy(e.z[0:r, i, chunks[c][0]:chunks[c][0] + n],
                                       e.bank[4 + j % 2][0:r, 0:n]).then_inc(s_zk, 1)
                for ct in range(4):
                    act.wait_ge(s_g, ct + 1)
                    nc.scalar.copy(e.convu[:, ct, CK - 1:SEQW], e.bank[ct % 2][:])
                    nc.scalar.copy(conv_s[:, ct, :, CK - 1:],
                                   e.bank[2 + ct % 2][:, 0:NS].rearrange("p (b t) -> p b t", b=NB)).then_inc(s_gk, 1)
                for ct in range(4):
                    act.wait_ge(s_g, ct + 5)
                    if ct >= 2:
                        act.wait_ge(s_gu, ct - 1)
                    nc.scalar.activation(eb[:, ct % 2, 0:SEQ], e.bank[ct % 2][:], ACT.Exp, scale=-1.0)
                    nc.scalar.activation(eb[:, ct % 2, SEQ:], e.bank[2 + ct % 2][:, 0:NS], ACT.Exp,
                                         scale=-1.0).then_inc(s_ge, 1)

            @block.vector
            def _(dve):
                link = Chain(dve, s_hc)
                nc.vector.memset(e.convu[:, :, 0:CK - 1], 0.0)
                for i in range(TILES):
                    r = rows(i)
                    s = 0 if i < PT else 1
                    dve.wait_ge(s_sq, i + 1)
                    nc.vector.tensor_scalar(rs[0:r, i:i + 1], ss[0:r, i:i + 1], 1.0 / D, EPS, ALU.mult,
                                            ALU.add).then_inc(s_var, 1)
                    dve.wait_ge(s_rs, i + 1)
                    link(nc.vector.reciprocal(rs[0:r, i:i + 1], rs[0:r, i:i + 1]))
                    link(nc.vector.scalar_tensor_tensor(ht[0:r, i % 2], xt[0:r, i % 2], rs[0:r, i:i + 1],
                                                        e.mods1[0:r, s, 1, :], ALU.mult, ALU.mult))
                    nc.vector.tensor_tensor(ht[0:r, i % 2], ht[0:r, i % 2], e.mods1[0:r, s, 0, :],
                                            ALU.add).then_inc(s_h, 1)
                dve.wait_ge(s_cT, 1)
                nc.vector.tensor_copy(e.cw[:].rearrange("p c k -> p (c k)"), e.bank[7][:, 0:4 * (CK + 1)]).then_inc(s_cK, 1)
                for a in range(2):
                    dve.wait_ge(s_cT, 2 + a)
                    ins = nc.vector.tensor_copy(conv_s[:, :, 4 * a:4 * a + 4, 0:CK - 1],
                                                e.bank[6 - 6 * a][:, 0:480].rearrange("p (c b w) -> p c b w", c=4, b=4))
                    ins.then_inc(s_cK, 1)
                for ct in range(4):
                    dve.wait_ge(s_ge, ct + 1)
                    g = eb[:, ct % 2]
                    link(nc.vector.tensor_scalar_add(g, g, 1.0))
                    link(nc.vector.reciprocal(g, g))
                    if ct == 0:
                        dve.wait_ge(s_gk, 4)
                    nc.vector.tensor_tensor(e.convu[:, ct, CK - 1:SEQW], e.convu[:, ct, CK - 1:SEQW], g[:, 0:SEQ],
                                            ALU.mult)
                    v = conv_s[:, ct, :, CK - 1:]
                    nc.vector.tensor_tensor(v, v, g[:, SEQ:].rearrange("p (b t) -> p b t", b=NB),
                                            ALU.mult).then_inc(s_gu, 1)
                dve.wait_ge(s_gu, 4)
                nc.vector.tensor_copy(usn[:].rearrange("p c (b t) -> p c b t", b=NB),
                                      conv_s[:, :, :, CK - 1:]).then_inc(s_un, 1)
                for q, r in enumerate((CK - 1, NS)):
                    dve.wait_ge(s_ut, q + 1)
                    nc.vector.tensor_copy(urow[0:r, q], e.bank[6 + q][0:r, :]).then_inc(s_uk, 1)

            @block.tensor
            def _(pe):
                for i in range(TILES):
                    r = rows(i)
                    pe.wait_ge(s_h, i + 1)
                    if i >= 2:
                        pe.wait_ge(s_hk, i - 1)
                    for k in range(KD):
                        last = nc.tensor.transpose(e.bank[2 * (i % 2) + k // 4][:, (k % 4) * r:(k % 4 + 1) * r],
                                                   ht[0:r, i % 2, k * P:(k + 1) * P], e.ident[0:r, 0:r])
                    last.then_inc(s_hT, 1)
                pe.wait_ge(s_cv, 64)
                for ct in range(4):
                    last = nc.tensor.transpose(e.bank[7][:, ct * 32:(ct + 1) * 32], cwr[:, ct * P:(ct + 1) * P],
                                               e.ident[0:CK + 1, 0:CK + 1])
                last.then_inc(s_cT, 1)
                pe.wait_ge(s_hk, TILES)
                for a in range(2):
                    for ct in range(4):
                        last = nc.tensor.transpose(e.bank[6 - 6 * a][:, ct * 120:(ct + 1) * 120],
                                                   hist[:, a, ct * P:(ct + 1) * P], e.ident[0:120, 0:120])
                    last.then_inc(s_cT, 1)
                for c in range(3):
                    pe.wait_ge(s_w[c % 2], 16 * (c // 2 + 1))
                    for i in range(TILES):
                        j = 5 * c + i
                        r, n = rows(i), chunks[c][1]
                        if j >= 2:
                            pe.wait_ge(s_zk, j - 1)
                        for k in range(KD):
                            last = nc.tensor.matmul(e.bank[4 + j % 2][0:r, 0:n], hT[:, k, i * P:i * P + r],
                                                    w[:, c % 2, k, 0:n], start=(k == 0), stop=(k == KD - 1))
                        last.then_inc(s_z, 1)
                pe.wait_ge(s_cK, 3)
                for c in range(2):
                    pe.wait_ge(s_w[(c + 3) % 2], 16 * ((c + 3) // 2 + 1))
                    for ct in range(4):
                        j = 4 * c + ct
                        if 2 <= j < 6:
                            pe.wait_ge(s_gk, j - 1)
                        if j >= 6:
                            pe.wait_ge(s_ge, j - 5)
                        for part, (o, n, b) in enumerate(((0, SEQ, 0), (SEQ, NS, 2))):
                            for k in range(KD):
                                last = nc.tensor.matmul(e.bank[b + ct % 2][:, 0:n],
                                                        w[:, (c + 3) % 2, k, ct * P:(ct + 1) * P],
                                                        hT[:, k, o:o + n], start=(k == 0), stop=(k == KD - 1))
                        last.then_inc(s_g, 1)
                pe.wait_ge(s_un, 1)
                for q in range(2):
                    for ct in range(4):
                        src = e.convu[:, ct, SEQ:SEQW] if q == 0 else usn[:, ct]
                        last = nc.tensor.transpose(e.bank[6 + q][0:src.shape[1], ct * P:(ct + 1) * P], src, e.ident)
                    last.then_inc(s_ut, 1)


def stage_qk(e):
    nc = e.nc
    with ExitStack() as ctx:
        NG = (KC - 0) // HD + 12
        sq = e.sb("z_squares", [P, 2, NG, HD], ctx=ctx)
        qr = e.sb("q_by_head_pair", [P, 2, R, G, HD], ctx=ctx)
        gs = e.sb("group_sums", [P, TILES, NG], ctx=ctx)
        gains = e.sb("qk_gains", [P, 4, HD], ctx=ctx)
        s_gn = e.sem("qk_gains_loaded")
        s_gc = e.sem("qk_gain_scaled")
        s_sq = e.sem("z_squared")
        s_qc = e.sem("qk_chain")
        s_var = e.sem("qk_variance")
        s_rs = e.sem("qk_rstd_ready")
        s_qn = e.sem("qk_normed")
        s_ge = e.sem("gate_exp")
        s_gt = e.sem("gates_ready")
        s_tr = e.sem("qk_transposed")
        s_tk = e.sem("qk_transposed_kept")
        s_wc = e.sem("window_copied")
        s_gd = e.sem("gates_to_dram")

        with nc.Block() as block:
            @block.sync
            def _(sp):
                sp.dma_start(gains[:, 0, :], e.q_norm.to_broadcast([P, HD])).then_inc(s_gn, 16)
                sp.dma_start(gains[:, 1:4, :].rearrange("p a d -> p (a d)"),
                             e.k_norm.rearrange("o a d -> o (a d)").to_broadcast([P, 3 * HD])).then_inc(s_gn, 16)
                outs_p = [(KC, e.new_cmp_prompt), (KS, e.new_sel_prompt), (KW, e.new_win_prompt)]
                outs_s = [(KC, e.new_cmp_sample), (KS, e.new_sel_sample)]
                sp.dma_start(e.new_win_sample[0, :, 0:WIN - DT].rearrange("b w a g d -> b w (a g d)"),
                             e.cache_win_kv[0, :, DT:].rearrange("b w a g d -> b w (a g d)")).then_inc(e.s_store, 16)
                e.stores += 1
                for i in range(TILES):
                    sp.wait_ge(s_qn, i + 1)
                    if i < PT:
                        for c, out in outs_p:
                            sp.dma_start(out.rearrange("o b s a g d -> (o b s) (a g d)")[i * P:(i + 1) * P],
                                         e.z[:, i, c:c + 2 * P]).then_inc(e.s_store, 16)
                            e.stores += 1
                    else:
                        for c, out in outs_s:
                            sp.dma_start(out.rearrange("o b s a g d -> (o b s) (a g d)"),
                                         e.z[0:NS, i, c:c + 2 * P]).then_inc(e.s_store, 16)
                            e.stores += 1
                        for b in range(NB):
                            sp.dma_start(e.new_win_sample[0, b, WIN - DT:].rearrange("w a g d -> w (a g d)"),
                                         e.z[b * DT:(b + 1) * DT, i, KW:KW + 2 * P]).then_inc(e.s_store, 16)
                            e.stores += 1
                sp.wait_ge(s_gt, TILES)
                sp.dma_start(e.gate_dram, e.gates[0:NS, PT, :]).then_inc(s_gd, 16)
                sp.wait_ge(s_gd, 16)
                for b in range(NB):
                    src = bass.AP(e.gate_dram.tensor, b * DT * 3 * H, [[3, H], [3 * H, DT], [1, 3]])
                    sp.dma_start(e.gates_s[b % 4 * 32:(b % 4 + 1) * 32, b // 4, :], src).then_inc(s_gd, 16)
                sp.wait_ge(s_gd, 16 * (NB + 1))
                sp.wait_ge(e.s_store, 16 * e.stores)

            def root(act, i):
                act.wait_ge(s_var, i + 1)
                r = rows(i)
                nc.scalar.activation(gs[0:r, i, :], gs[0:r, i, :], ACT.Sqrt).then_inc(s_rs, 1)

            @block.scalar
            def _(act):
                for i in range(TILES):
                    r = rows(i)
                    nc.scalar.activation(e.gates[0:r, i, :], e.z[0:r, i, NG * HD:ROWCOLS], ACT.Exp,
                                         scale=-1.0).then_inc(s_ge, 1)
                for i in range(TILES):
                    r = rows(i)
                    if i >= 2:
                        act.wait_ge(s_var, i - 1)
                    nc.scalar.activation(sq[0:r, i % 2].rearrange("p g d -> p (g d)"), e.z[0:r, i, 0:NG * HD],
                                         ACT.Square).then_inc(s_sq, 1)
                    if i >= 1:
                        root(act, i - 1)
                root(act, TILES - 1)

            def keep(dve, i):
                dve.wait_ge(s_tr, i + 1)
                r = rows(i)
                b0, b1 = e.bank[2 * (i % 2)], e.bank[2 * (i % 2) + 1]
                if i < PT:
                    nc.vector.tensor_copy(e.qT[:, i, :, :].rearrange("p r n -> p (r n)"), b0[:])
                    nc.vector.tensor_copy(e.ksT[:, i * P:(i + 1) * P], b1[:, 0:P])
                    nc.vector.tensor_copy(e.kwT[:, i * P:(i + 1) * P], b1[:, P:2 * P]).then_inc(s_tk, 1)
                else:
                    qp = e.qpad[:].rearrange("p b (s g r t) -> p b s g r t", s=4, g=G, r=R)
                    for g in range(G):
                        for b in range(NB):
                            src = b0[g * HD:(g + 1) * HD, 0:R * NS].rearrange("p (r b t) -> p b r t", r=R, b=NB)
                            nc.vector.tensor_copy(qp[g * HD:(g + 1) * HD, b, b % 4, g], src[:, b])
                            nc.vector.tensor_copy(
                                e.qall[g * HD:(g + 1) * HD, b // 4, :].rearrange(
                                    "p (s g r t) -> p s g r t", s=4, g=G, r=R)[:, b % 4, g], src[:, b])
                            nc.vector.memset(
                                e.qall[(1 - g) * HD:(2 - g) * HD, b // 4, :].rearrange(
                                    "p (s g r t) -> p s g r t", s=4, g=G, r=R)[:, b % 4, g], 0.0)
                    nc.vector.tensor_copy(e.newT[:, 0, :], b1[:, 0:NS])
                    nc.vector.tensor_copy(e.newT[:, 1, :], b1[:, NS:2 * NS]).then_inc(s_tk, 1)

            @block.vector
            def _(dve):
                link = Chain(dve, s_qc)
                dve.wait_ge(s_gn, 32)
                link(nc.vector.tensor_scalar_mul(gains[:, 0, :], gains[:, 0, :], HD ** -0.5))
                link(nc.vector.memset(e.qpad[:], 0.0))
                for i in range(TILES):
                    r = rows(i)
                    dve.wait_ge(s_sq, i + 1)
                    link(nc.vector.tensor_reduce(gs[0:r, i, :], sq[0:r, i % 2], AX, ALU.add))
                    nc.vector.tensor_scalar(gs[0:r, i, :], gs[0:r, i, :], 1.0 / HD, EPS, ALU.mult,
                                            ALU.add).then_inc(s_var, 1)
                    dve.wait_ge(s_rs, i + 1)
                    link(nc.vector.reciprocal(gs[0:r, i, :], gs[0:r, i, :]))
                    parts = [(0, H, 0), (KS // HD, G, 2), (KW // HD, G, 3)]
                    zg = e.z[0:r, i, 0:NG * HD].rearrange("p (g d) -> p g d", d=HD)
                    for g0, n, _ in parts:
                        last = nc.vector.tensor_tensor(zg[:, g0:g0 + n], zg[:, g0:g0 + n],
                                                       span(gs[0:r, i, g0:g0 + n], 2, HD), ALU.mult)
                    link(last)
                    dve.wait_ge(s_ge, i + 1)
                    link(nc.vector.tensor_scalar_add(e.gates[0:r, i, :], e.gates[0:r, i, :], 1.0))
                    nc.vector.reciprocal(e.gates[0:r, i, :], e.gates[0:r, i, :]).then_inc(s_gt, 1)
                    if i >= 2:
                        dve.wait_ge(s_tr, i - 1)
                    for g in range(G):
                        nc.vector.tensor_tensor(qr[0:r, i % 2, :, g, :], zg[:, g * R:(g + 1) * R],
                                                span(gains[0:r, 0, :], 1, R), ALU.mult)
                    for g0, n, a in parts[1:]:
                        last = nc.vector.tensor_tensor(zg[:, g0:g0 + n], zg[:, g0:g0 + n],
                                                       span(gains[0:r, a, :], 1, n), ALU.mult)
                    last.then_inc(s_qn, 1)
                    if i >= 1:
                        keep(dve, i - 1)
                keep(dve, TILES - 1)

            @block.tensor
            def _(pe):
                for i in range(TILES):
                    r = rows(i)
                    pe.wait_ge(s_qn, i + 1)
                    if i >= 2:
                        pe.wait_ge(s_tk, i - 1)
                    b0, b1 = e.bank[2 * (i % 2)], e.bank[2 * (i % 2) + 1]
                    for q in range(R):
                        src = qr[0:r, i % 2, q].rearrange("p g d -> p (g d)")
                        nc.tensor.transpose(b0[:, q * r:(q + 1) * r], src, e.ident[0:r, 0:r])
                    nc.tensor.transpose(b1[:, 0:r], e.z[0:r, i, KS:KS + P], e.ident[0:r, 0:r])
                    nc.tensor.transpose(b1[:, r:2 * r], e.z[0:r, i, KW:KW + P], e.ident[0:r, 0:r]).then_inc(s_tr, 1)

def stage_compress(e, kv):
    nc = e.nc
    which = "kv"[kv]
    NCH = NB * PAST // 16 + SEQ // 16
    NPC = NCH - NB * PAST // 16
    NHID = NB * NC_S + NC_P
    with ExitStack() as ctx:
        raw = e.sb(f"pages_{which}", [P, 2, PAGES // 2, 2, P], ctx=ctx)
        pairs = e.sb(f"pairs_{which}", [P, 2, PAGES // 2, G, 2, HD], ctx=ctx)
        rT = e.sb(f"chunks_{which}", [P, G, 8, NCH], ctx=ctx)
        w1 = e.sb(f"cmp_w1_{which}", [P, 16, CMP_HID], ctx=ctx)
        w2 = e.sb(f"cmp_w2_{which}", [P, 2, HD], ctx=ctx)
        b2 = e.sb(f"cmp_b2_{which}", [P, HD], ctx=ctx)
        gain = e.sb(f"cmp_gain_{which}", [P, HD], ctx=ctx)
        per = e.sb(f"cmp_pe_rows_{which}", [18, P], ctx=ctx)
        peT = e.sb(f"cmp_pe_{which}", [P, 18], ctx=ctx)
        hb = e.sb(f"cmp_hidden_bias_{which}", [P, 2], ctx=ctx)
        hid = e.sb(f"cmp_hidden_{which}", [P, G, 2, NHID], ctx=ctx)
        ptab = e.sb(f"page_ids_{which}", [1, NB * PAGES], I32, ctx=ctx)
        NR = NB * G + G
        crow = e.sb(f"cmp_rows_{which}", [NC_S, NR, HD], ctx=ctx)
        csum = e.sb(f"cmp_sums_{which}", [NC_S, NR], ctx=ctx)

        def sem(name):
            return e.sem(f"{name}_{which}")

        s_pt = sem("page_ids_loaded")
        s_w = sem("cmp_weights_loaded")
        s_raw = [sem(f"pages_loaded{i}") for i in range(2)]
        s_pk = [sem(f"pages_packed{i}") for i in range(2)]
        s_tr = sem("pairs_transposed")
        s_tk = [sem(f"chunks_kept_g{i}") for i in range(G)]
        s_pe = sem("pe_transposed")
        s_pek = sem("pe_kept")
        s_hb = sem("pe_product")
        s_hbk = sem("hidden_bias_ready")
        s_h = sem("hidden_product")
        s_hk = sem("hidden_kept")
        s_o = sem("cmp_rows_product")
        s_ch = sem("cmp_chain")
        s_sq = sem("cmp_var_ready")
        s_rt = sem("cmp_root_ready")
        s_n = sem("cmp_rows_normed")
        s_ct = sem("cmp_transposed")

        SEQS = NB + 1
        cache = e.cache_cmp_kv[0].rearrange("n (q s) a g d -> n q s a (g d)", s=2)
        mine = e.new_cmp_prompt[0, 0].rearrange("(t q s) a g d -> t q s a (g d)", t=2, s=2)

        with nc.Block() as block:
            @block.sync
            def _(sp):
                sp.dma_start(ptab[:], e.page_table.rearrange("(o b) p -> o (b p)", o=1)).then_inc(s_pt, 16)
                sp.wait_ge(s_pt, 16)
                with sp.Fori(0, NB // 2) as bb:
                    for slot in range(2):
                        sp.wait_ge(s_pk[slot], bb + 1)
                        for p in range(PAGES):
                            page = sp.value_load(ptab[0:1, bass.ds(bb * (2 * PAGES) + (slot * PAGES + p), 1)],
                                                 min_val=0, max_val=e.cache_cmp_kv.shape[1] - 1)
                            src = cache[bass.ds(page, 1), :, :, kv, :].rearrange("o q s c -> (o q) s c")
                            sp.dma_start(raw[(p % 2) * 64:(p % 2 + 1) * 64, slot, p // 2], src
                                         ).then_inc(s_raw[slot], 16)
                sp.wait_ge(s_pk[0], NB // 2 + 1)
                for t in range(2):
                    sp.dma_start(raw[:, 0, t], mine[t, :, :, kv, :]).then_inc(s_raw[0], 16)

            @block.scalar
            def _(act):
                act.dma_start(per[0:16, :], e.cmp_pe[0, kv].rearrange("(k s) d -> k (s d)", s=2)).then_inc(s_w, 16)
                act.dma_start(per[16:18, :], e.cmp_b1[0, kv:kv + 1].rearrange("o (a n) -> (o a) n", a=2)).then_inc(s_w, 16)
                act.dma_start(w1[:], e.cmp_w1[0, kv].rearrange("(k p) n -> p k n", p=P)).then_inc(s_w, 16)
                act.dma_start(w2[:], e.cmp_w2[0, kv].rearrange("(k p) n -> p k n", p=P)).then_inc(s_w, 16)
                act.dma_start(b2[:], e.cmp_b2[0, kv:kv + 1].to_broadcast([P, HD])).then_inc(s_w, 16)
                act.dma_start(gain[:], e.k_norm[0, 0:1].to_broadcast([P, HD])).then_inc(s_w, 16)
                for b in range(SEQS):
                    act.wait_ge(s_tr, b + 1)
                    n = 64 if b < NB else NPC
                    nc.scalar.copy(rT[:, 0, :, b * 64:b * 64 + n],
                                   e.bank[2 * (b % 2)][:, 0:8 * n].rearrange("p (c s) -> p s c", s=8)
                                   ).then_inc(s_tk[0], 1)
                act.wait_ge(s_hbk, 1)
                for g in range(G):
                    for hh in range(2):
                        j = 2 * g + hh
                        act.wait_ge(s_h, j + 1)
                        nc.scalar.activation(hid[:, g, hh, 0:NB * NC_S], e.bank[4 + 2 * (j % 2)][:, 0:NB * NC_S],
                                             ACT.Gelu_apprx_tanh, bias=hb[:, hh:hh + 1])
                        nc.scalar.activation(hid[:, g, hh, NB * NC_S:], e.bank[5 + 2 * (j % 2)][:, 0:NC_P],
                                             ACT.Gelu_apprx_tanh, bias=hb[:, hh:hh + 1]).then_inc(s_hk, 1)
                if kv == 0:
                    act.wait_ge(s_sq, 1)
                    nc.scalar.activation(csum[:], csum[:], ACT.Sqrt).then_inc(s_rt, 1)

            @block.gpsimd
            def _(pool):
                for slot in range(2):
                    pool.sem_inc(s_pk[slot], 1)
                for b in range(SEQS):
                    slot = b % 2
                    pool.wait_ge(s_raw[slot], 16 * PAGES * (b // 2 + 1) if b < NB else 16 * (PAGES * NB // 2 + 2))
                    if b >= 2:
                        pool.wait_ge(s_tr, b - 1)
                    n = PAGES // 2 if b < NB else 2
                    for t in range(n):
                        last = nc.gpsimd.tensor_copy(pairs[:, slot, t],
                                                     raw[:, slot, t].rearrange("p s (g d) -> p g s d", g=G))
                    last.then_inc(s_pk[slot], 1)

            @block.vector
            def _(dve):
                link = Chain(dve, s_ch)
                dve.wait_ge(s_pe, 1)
                nc.vector.tensor_copy(peT[:], e.bank[7][:, 0:18]).then_inc(s_pek, 1)
                dve.wait_ge(s_hb, 1)
                nc.vector.tensor_tensor(hb[:], e.bank[6][:, 0:2], peT[:, 16:18], ALU.add).then_inc(s_hbk, 1)
                for b in range(SEQS):
                    dve.wait_ge(s_tr, b + 1)
                    n = 64 if b < NB else NPC
                    nc.vector.tensor_copy(rT[:, 1, :, b * 64:b * 64 + n],
                                          e.bank[2 * (b % 2) + 1][:, 0:8 * n].rearrange("p (c s) -> p s c", s=8)
                                          ).then_inc(s_tk[1], 1)
                dve.wait_ge(s_o, 1)
                if kv == 0:
                    link(nc.vector.memset(crow[:], 0.0))
                    for half in range(2):
                        nc.vector.tensor_tensor(crow[:, half * 8:(half + 1) * 8, :],
                                                e.bank[half][0:NC_S, :].rearrange("p (g d) -> p g d", d=HD),
                                                span(b2[0:NC_S, :], 1, 8), ALU.add)
                    link(nc.vector.tensor_tensor(crow[0:NC_P, 16:18, :],
                                                 e.bank[2][0:NC_P, 0:P].rearrange("p (g d) -> p g d", d=HD),
                                                 span(b2[0:NC_P, :], 1, G), ALU.add))
                    sq = hid[0:NC_S].rearrange("p g a n -> p (g a n)")[:, 0:NR * HD].rearrange(
                        "p (r d) -> p r d", d=HD)
                    link(nc.vector.tensor_tensor(sq, crow[:], crow[:], ALU.mult))
                    link(nc.vector.tensor_reduce(csum[:], sq, AX, ALU.add))
                    nc.vector.tensor_scalar(csum[:], csum[:], 1.0 / HD, EPS, ALU.mult, ALU.add).then_inc(s_sq, 1)
                    dve.wait_ge(s_rt, 1)
                    link(nc.vector.reciprocal(csum[:], csum[:]))
                    link(nc.vector.tensor_tensor(crow[:], crow[:], span(csum[:], 2, HD), ALU.mult))
                    nc.vector.tensor_tensor(crow[:], crow[:], span(gain[0:NC_S, :], 1, NR), ALU.mult).then_inc(s_n, 1)
                    dve.wait_ge(s_ct, 1)
                    nc.vector.tensor_copy(e.kcT_s[:].rearrange("p b c -> p (b c)"), e.bank[3][:, 0:NB * NC_S])
                    nc.vector.tensor_copy(e.kcT_p[:], e.bank[5][:, 0:NC_P])
                else:
                    for half in range(2):
                        nc.vector.tensor_tensor(
                            e.vc_s[:, half * 4:(half + 1) * 4, :].rearrange("p b (g d) -> p (b g) d", d=HD),
                            e.bank[half][0:NC_S, :].rearrange("p (g d) -> p g d", d=HD),
                            span(b2[0:NC_S, :], 1, 8), ALU.add)
                    nc.vector.tensor_tensor(e.vc_p[:].rearrange("p (g d) -> p g d", d=HD),
                                            e.bank[2][0:NC_P, 0:P].rearrange("p (g d) -> p g d", d=HD),
                                            span(b2[0:NC_P, :], 1, G), ALU.add)

            @block.tensor
            def _(pe):
                pe.wait_ge(s_w, 96)
                nc.tensor.transpose(e.bank[7][:, 0:18], per[:], e.ident[0:18, 0:18]).then_inc(s_pe, 1)
                pe.wait_ge(s_pek, 1)
                for hh in range(2):
                    for k in range(16):
                        last = nc.tensor.matmul(e.bank[6][:, hh:hh + 1], w1[:, k, hh * P:(hh + 1) * P], peT[:, k:k + 1],
                                                start=(k == 0), stop=(k == 15))
                last.then_inc(s_hb, 1)
                for b in range(SEQS):
                    slot = b % 2
                    pe.wait_ge(s_pk[slot], b // 2 + 2)
                    if b >= 2:
                        pe.wait_ge(s_tk[0], b - 1)
                        pe.wait_ge(s_tk[1], b - 1)
                    for g in range(G):
                        for t in range(PAGES // 2 if b < NB else 2):
                            last = nc.tensor.transpose(e.bank[2 * (b % 2) + g][:, t * P:(t + 1) * P],
                                                       pairs[:, slot, t, g].rearrange("p s d -> p (s d)"), e.ident)
                    last.then_inc(s_tr, 1)
                pe.wait_ge(s_tk[0], SEQS)
                pe.wait_ge(s_tk[1], SEQS)
                pe.wait_ge(s_hbk, 1)
                for g in range(G):
                    for hh in range(2):
                        j = 2 * g + hh
                        if j >= 2:
                            pe.wait_ge(s_hk, j - 1)
                        for part in range(2):
                            for k in range(16):
                                one, s = k // 8, k % 8
                                if part == 0:
                                    rhs = rT[:, g, s, 0:NB * 64].rearrange("p (b c) -> p b c", b=NB)[:, :, one:one + NC_S]
                                    out = e.bank[4 + 2 * (j % 2)][:, 0:NB * NC_S]
                                else:
                                    rhs = rT[:, g, s, NB * 64 + one:NB * 64 + one + NC_P]
                                    out = e.bank[5 + 2 * (j % 2)][:, 0:NC_P]
                                last = nc.tensor.matmul(out, w1[:, k, hh * P:(hh + 1) * P], rhs,
                                                        start=(k == 0), stop=(k == 15))
                        last.then_inc(s_h, 1)
                pe.wait_ge(s_hk, 4)
                for g in range(G):
                    for b in range(SEQS):
                        n = NC_S if b < NB else NC_P
                        bank = e.bank[b // 4]
                        c = (b % 4) * P + g * HD
                        for hh in range(2):
                            last = nc.tensor.matmul(bank[0:n, c:c + HD], hid[:, g, hh, b * NC_S:b * NC_S + n],
                                                    w2[:, hh, :], start=(hh == 0), stop=(hh == 1))
                last.then_inc(s_o, 1)
                if kv == 0:
                    pe.wait_ge(s_n, 1)
                    for b in range(SEQS):
                        n = NC_S if b < NB else NC_P
                        out = e.bank[3][:, b * NC_S:(b + 1) * NC_S] if b < NB else e.bank[5][:, 0:NC_P]
                        last = nc.tensor.transpose(out, crow[0:n, 2 * b:2 * b + 2, :].rearrange("p g d -> p (g d)"),
                                                   e.ident[0:n, 0:n])
                    last.then_inc(s_ct, 1)

def stage_prompt(e):
    nc = e.nc
    units = [(qt, h, br) for qt in range(PT) for h in range(H) for br in range(3)]
    U = len(units)

    def keys(qt, br):
        return 8 * qt + 7 if br == 0 else (qt + 1) * P

    with ExitStack() as ctx:
        L = e.sb("logits", [P, 3, SEQ], ctx=ctx)
        ET = e.sb("probs_transposed", [P, 2, 4, P], ctx=ctx)
        m = e.sb("row_max", [P, 3], ctx=ctx)
        nm = e.sb("row_shift", [P, 3], ctx=ctx)
        den = e.sb("row_sums", [P, 2, 3, H], ctx=ctx)
        coef = e.sb("branch_weights", [P, 3, H], ctx=ctx)
        part = e.sb("branch_parts", [P, 3, AW], ctx=ctx)

        s_s = e.sem("scores_ready")
        s_l = e.sem("logits_ready")
        s_m = e.sem("shift_ready")
        s_e = e.sem("probs_ready")
        s_t = e.sem("probs_turned")
        s_tk = e.sem("probs_turned_kept")
        s_o = e.sem("unit_output")
        s_c = e.sem("tile_combined")
        s_ch = e.sem("prompt_chain")
        tap = e.tap
        s_cv = e.s_conv = e.sem("conv_steps_gpsimd")
        s_cp = e.sem("tap_products_ready")
        s_cd = e.sem("conv_steps_vector")

        with nc.Block(no_gpsimd_drain=True) as block:
            @block.gpsimd
            def _(pool):
                ct = 3
                src = e.convu[:, ct]
                nc.gpsimd.tensor_scalar(e.convo[:, ct], src[:, 0:CONVO], e.cw[:, ct, 0:1], e.cw[:, ct, CK:CK + 1],
                                        ALU.mult, ALU.add).then_inc(s_cv, 1)
                for k in range(1, CK):
                    if k >= 3:
                        pool.wait_ge(s_cv, k - 1)
                    nc.gpsimd.tensor_scalar_mul(tap[:, k % 2], src[:, k:k + CONVO], e.cw[:, ct, k:k + 1]).then_inc(s_cp, 1)
                    pool.wait_ge(s_cp, k)
                    pool.wait_ge(s_cv, k)
                    nc.gpsimd.tensor_tensor(e.convo[:, ct], e.convo[:, ct], tap[:, k % 2], ALU.add).then_inc(s_cv, 1)

            @block.scalar
            def _(act):
                for u, (qt, h, br) in enumerate(units):
                    n = keys(qt, br)
                    act.wait_ge(s_m, u + 1)
                    if h == 0 and br == 0 and qt > 1:
                        act.wait_ge(s_c, qt - 1)
                    nc.scalar.activation(L[:, u % 3, 0:n], L[:, u % 3, 0:n], ACT.Exp, bias=nm[:, u % 3:u % 3 + 1],
                                         accum_out=den[:, qt % 2, br, h:h + 1]).then_inc(s_e, 1)

            @block.vector
            def _(dve):
                link = Chain(dve, s_ch)

                def keep(u):
                    qt, h, br = units[u]
                    n = keys(qt, br)
                    dve.wait_ge(s_t, u + 1)
                    if u >= 2:
                        dve.wait_ge(s_o, u - 1)
                    k = min(n, P)
                    blocks = max(1, n // P)
                    nc.vector.tensor_copy(ET[0:k, u % 2, 0:blocks, :],
                                          e.bank[2 + u % 2][0:k, 0:blocks * P].rearrange("p (b q) -> p b q", q=P)
                                          ).then_inc(s_tk, 1)
                    if (h, br) == (H - 1, 2):
                        combine(qt)

                def tap_step(n):
                    k, ct = n // 3, n % 3
                    if k == 0:
                        ins = nc.vector.tensor_scalar(e.convo[:, ct], e.convu[:, ct, 0:CONVO], e.cw[:, ct, 0:1],
                                                      e.cw[:, ct, CK:CK + 1], ALU.mult, ALU.add)
                    else:
                        dve.wait_ge(s_cd, n - 2)
                        ins = nc.vector.scalar_tensor_tensor(e.convo[:, ct], e.convu[:, ct, k:k + CONVO],
                                                             e.cw[:, ct, k:k + 1], e.convo[:, ct], ALU.mult, ALU.add)
                    ins.then_inc(s_cd, 1)

                def combine(qt):
                    gate = e.gates[:, qt, :].rearrange("p (h b) -> p b h", b=3)
                    dve.wait_ge(s_e, 24 * (qt + 1))
                    link(nc.vector.tensor_scalar_max(coef[:], den[:, qt % 2], 1e-30))
                    link(nc.vector.reciprocal(coef[:], coef[:]))
                    link(nc.vector.tensor_tensor(coef[:], coef[:], gate, ALU.mult))
                    dve.wait_ge(s_o, 24 * (qt + 1))
                    for br in range(3):
                        last = nc.vector.tensor_tensor(part[:, br].rearrange("p (h d) -> p h d", h=H),
                                                       e.bank[4 + br][:].rearrange("p (h d) -> p h d", h=H),
                                                       span(coef[:, br], 2, HD), ALU.mult)
                    link(last)
                    link(nc.vector.tensor_tensor(part[:, 0], part[:, 0], part[:, 1], ALU.add))
                    nc.vector.tensor_tensor(e.attn[:, qt], part[:, 0], part[:, 2], ALU.add).then_inc(s_c, 1)

                for u, (qt, h, br) in enumerate(units):
                    n = keys(qt, br)
                    dve.wait_ge(s_s, u + 1)
                    if u >= 3:
                        dve.wait_ge(s_t, u - 2)
                    if br == 0:
                        c = SEQ - P - P * qt + 31
                        bias = e.bias_p[:, h, c:c + 16 * (n - 1) + 1:16]
                    else:
                        bias = e.bias_p[:, h, SEQ - n:SEQ]
                    nc.vector.tensor_tensor_reduce(out=L[:, u % 3, 0:n], in0=e.bank[u % 2][:, 0:n], in1=bias,
                                                   scale=1.0, scalar=NEG, op0=ALU.add, op1=ALU.max,
                                                   accum_out=m[:, u % 3:u % 3 + 1]).then_inc(s_l, 1)
                    dve.wait_ge(s_l, u + 1)
                    nc.vector.tensor_scalar(nm[:, u % 3:u % 3 + 1], m[:, u % 3:u % 3 + 1], NEG / 10, -1.0,
                                            ALU.max, ALU.mult).then_inc(s_m, 1)
                    if u >= 1:
                        keep(u - 1)
                    if u < 3 * CK:
                        tap_step(u)
                keep(U - 1)

            @block.tensor
            def _(pe):
                def scores(u):
                    qt, h, br = units[u]
                    g, n = h // R, keys(qt, br)
                    lo = g * HD
                    kT = (e.kcT_p, e.ksT, e.kwT)[br]
                    if u >= 2:
                        pe.wait_ge(s_l, u - 1)
                    nc.tensor.matmul(e.bank[u % 2][:, 0:n], e.qT[lo:lo + HD, qt, h % R, :], kT[lo:lo + HD, 0:n],
                                     start=True, stop=True).then_inc(s_s, 1)

                def turn(u):
                    qt, h, br = units[u]
                    n = keys(qt, br)
                    pe.wait_ge(s_e, u + 1)
                    if u >= 2:
                        pe.wait_ge(s_tk, u - 1)
                    for j in range(max(1, n // P)):
                        k = min(n, P)
                        last = nc.tensor.transpose(e.bank[2 + u % 2][0:k, j * P:(j + 1) * P],
                                                   L[:, u % 3, j * P:j * P + k], e.ident)
                    last.then_inc(s_t, 1)

                def output(u):
                    qt, h, br = units[u]
                    g, n = h // R, keys(qt, br)
                    pe.wait_ge(s_tk, u + 1)
                    if qt > 0 and (h, br) == (0, 0):
                        pe.wait_ge(s_c, qt)
                    blocks = max(1, n // P)
                    for j in range(blocks):
                        k = min(n, P)
                        v = (e.vc_p[0:k, g * HD:(g + 1) * HD] if br == 0 else
                             e.z[:, j, (VS, VW)[br - 1] + g * HD:(VS, VW)[br - 1] + (g + 1) * HD])
                        last = nc.tensor.matmul(e.bank[4 + br][:, h * HD:(h + 1) * HD], ET[0:k, u % 2, j, :], v,
                                                start=(j == 0), stop=(j == blocks - 1))
                    last.then_inc(s_o, 1)

                for s in range(U + 2):
                    if s < U:
                        scores(s)
                    if 0 <= s - 1 < U:
                        turn(s - 1)
                    if s - 2 >= 0:
                        output(s - 2)


def stage_sample(e):
    nc = e.nc
    with ExitStack() as ctx:
        selr = e.sb("sel_pages", [P, 4, PAGES, 2 * P], ctx=ctx)
        winr = e.sb("win_rows", [P, 4, WIN // P, 2 * P], ctx=ctx)
        ptab = e.sb("sel_page_ids", [1, NB * PAGES], I32, ctx=ctx)
        kT = e.qT[:].rearrange("p a b c -> p (a b c)").rearrange("p (s n) -> p s n", s=2)
        room = e.bias_p[:].rearrange("p a b -> p (a b)")
        lsel = room[:, 0:PAST + NS]
        lwin = room[:, PAST + NS:PAST + NS + WIN + NS]
        o = PAST + NS + WIN + NS
        NT = 15
        PTt = room[:, o:o + NT * P].rearrange("p (a q) -> p a q", a=NT)
        o += NT * P
        pc = room[:, o:o + 72]
        blk = e.sb("block_sums", [P, NSEL], ctx=ctx)
        key = e.sb("drop_key", [P, NSEL], ctx=ctx)
        dmask = e.sb("drop_mask", [P, NSEL], ctx=ctx)
        st = e.sb("sample_stats", [P, 16], ctx=ctx)
        oS = e.sb("sample_out", [P, H, 2, 4, DT], ctx=ctx)

        s_pt = e.sem("sel_page_ids_loaded")
        s_selr = [e.sem(f"sel_pages_loaded{i}") for i in range(4)]
        s_winr = [e.sem(f"win_rows_loaded{i}") for i in range(4)]
        s_kt = e.sem("keys_turned")
        s_kk = e.sem("keys_kept")
        s_ks = e.sem("keys_used")
        s_sc = e.sem("sample_scores")
        s_lc = e.sem("sample_logits_read")
        s_ch = e.sem("sample_chain")
        s_nm = e.sem("sample_shift")
        s_ex = e.sem("sample_exp")
        s_bs = e.sem("block_sums_ready")
        s_im = e.sem("importance_ready")
        s_p = e.sem("sample_probs")
        s_pT = e.sem("sample_probs_turned")
        s_pk = e.sem("sample_probs_kept")
        s_o = e.sem("sample_output")
        s_ok = e.sem("sample_output_kept")
        s_or = e.sem("sample_rows_turned")

        cache = e.cache_sel_kv[0].rearrange("n s a g d -> n s (a g d)")
        SB, WB, CB, NBK, OB = e.bank[0:2], e.bank[2], e.bank[3], e.bank[4], e.bank[7]

        with nc.Block(no_gpsimd_drain=True) as block:
            @block.sync
            def _(sp):
                sp.dma_start(ptab[:], e.page_table.rearrange("(o b) p -> o (b p)", o=1)).then_inc(s_pt, 16)
                sp.wait_ge(s_pt, 16)
                with sp.Fori(0, 2) as hi:
                    for b4 in range(4):
                        sp.wait_ge(s_o, hi + 1)
                        for p in range(PAGES):
                            page = sp.value_load(ptab[0:1, bass.ds(hi * (4 * PAGES) + (b4 * PAGES + p), 1)],
                                                 min_val=0, max_val=e.cache_sel_kv.shape[1] - 1)
                            sp.dma_start(selr[:, b4, p], cache[bass.ds(page, 1)].rearrange("o s c -> (o s) c")
                                         ).then_inc(s_selr[b4], 16)

            @block.scalar
            def _(act):
                for hi in range(2):
                    if hi:
                        act.wait_ge(s_o, 2)
                    for b4 in range(4):
                        act.dma_start(winr[:, b4], e.cache_win_kv[0, 4 * hi + b4].rearrange(
                            "(j s) a g d -> s j (a g d)", s=P)).then_inc(s_winr[b4], 16)
                    for b4 in range(4):
                        for q in range(3):
                            j = (4 * hi + b4) * 3 + q
                            act.wait_ge(s_kt, j + 1)
                            if j >= 4:
                                act.wait_ge(s_ks, j - 3)
                            nc.scalar.copy(kT[:, (j % 4) // 2, j % 2 * 512:(j % 2 + 1) * 512],
                                           e.bank[5 + j % 2][:]).then_inc(s_kk, 1)
                    d = 8
                    for q, l in enumerate((pc[:, 1:1 + NC_S], lsel, lwin)):
                        act.wait_ge(s_nm, 3 * hi + q + 1)
                        nc.scalar.activation(l, l, ACT.Exp, bias=st[:, 4 + q:5 + q],
                                             accum_out=st[:, d + q:d + q + 1]).then_inc(s_ex, 1)

            @block.vector
            def _(dve):
                link = Chain(dve, s_ch)
                iota = e.consts[:, C_IOTA:C_IOTA + NSEL]
                for hi in range(2):
                    link(nc.vector.memset(pc[:], 0.0))
                    link(nc.vector.memset(dmask[:], 0.0))
                    dve.wait_ge(s_sc, hi + 1)

                    def shift(q, l):
                        link(nc.vector.tensor_reduce(st[:, q:q + 1], l, AX, ALU.max))
                        nc.vector.tensor_scalar_mul(st[:, 4 + q:5 + q], st[:, q:q + 1], -1.0).then_inc(s_nm, 1)

                    lc = pc[:, 1:1 + NC_S]
                    link(nc.vector.tensor_tensor(lc, CB[:, 0:NC_S], e.bias_s[:, 31:PAST:16], ALU.add))
                    shift(0, lc)
                    nc.vector.tensor_tensor(lwin[:, 0:WIN], WB[:], e.bias_w[:], ALU.add)
                    link(nc.vector.tensor_tensor(lwin[:, WIN:], NBK[:, NS:2 * NS],
                                                 e.bias_new[:, hi].rearrange("p b t -> p (b t)"), ALU.add))
                    for c in range(2):
                        nc.vector.tensor_tensor(lsel[:, c * 512:(c + 1) * 512], SB[c][:],
                                                e.bias_s[:, c * 512:(c + 1) * 512], ALU.add)
                    link(nc.vector.tensor_tensor(lsel[:, PAST:], NBK[:, 0:NS],
                                                 e.bias_new[:, hi].rearrange("p b t -> p (b t)"), ALU.add))
                    dve.wait_ge(s_ex, 3 * hi + 1)
                    link(nc.vector.reciprocal(st[:, 12:13], st[:, 8:9]))
                    link(nc.vector.tensor_scalar_mul(lc, lc, st[:, 12:13]))
                    link(nc.vector.tensor_reduce(blk[:], pc[:, 0:4 * NSEL].rearrange("p (j c) -> p j c", c=4), AX,
                                                 ALU.add))
                    nc.vector.tensor_tensor(blk[:], blk[:], pc[:, 4:4 * NSEL + 1:4], ALU.add).then_inc(s_bs, 1)
                    dve.wait_ge(s_im, hi + 1)
                    imp = NBK[:, 64 + 1:64 + NSEL - 2]
                    kk = key[:, 1:NSEL - 2]
                    link(nc.vector.tensor_reduce(st[:, 13:14], imp, AX, ALU.min))
                    link(nc.vector.scalar_tensor_tensor(kk, imp, st[:, 13:14], iota[:, 1:NSEL - 2],
                                                        ALU.is_equal, ALU.mult))
                    link(nc.vector.tensor_reduce(st[:, 14:15], kk, AX, ALU.max))
                    link(nc.vector.tensor_scalar(dmask[:, 1:NSEL - 2], kk, st[:, 14:15], NEG, ALU.is_equal, ALU.mult))
                    old = lsel[:, 0:PAST].rearrange("p (j c) -> p j c", c=64)
                    link(nc.vector.tensor_tensor(old, old, span(dmask[:, 0:NSEL - 1], 2, 64), ALU.add))
                    shift(1, lsel)
                    shift(2, lwin)
                    nc.vector.tensor_scalar_mul(lc, lc, e.gates_s[:, hi, 0:1]).then_inc(s_p, 1)
                    for q, l in ((1, lsel), (2, lwin)):
                        dve.wait_ge(s_ex, 3 * hi + q + 1)
                        link(nc.vector.reciprocal(st[:, 12 + q:13 + q], st[:, 8 + q:9 + q]))
                        link(nc.vector.tensor_tensor(st[:, 12 + q:13 + q], st[:, 12 + q:13 + q],
                                                     e.gates_s[:, hi, q:q + 1], ALU.mult))
                        nc.vector.tensor_scalar_mul(l, l, st[:, 12 + q:13 + q]).then_inc(s_p, 1)
                    for q in range(4):
                        dve.wait_ge(s_pT, 4 * hi + q + 1)
                        n = min(4, NT - 4 * q)
                        src = e.bank[5 + q % 2]
                        if q == 0:
                            nc.vector.tensor_copy(PTt[0:NC_S, 0], src[0:NC_S, 0:P])
                            ins = nc.vector.tensor_copy(PTt[:, 1:4], src[:, P:].rearrange("p (a q) -> p a q", q=P))
                        elif q < 3:
                            ins = nc.vector.tensor_copy(PTt[:, 4 * q:4 * q + 4], src[:].rearrange("p (a q) -> p a q", q=P))
                        else:
                            nc.vector.tensor_copy(PTt[:, 12], src[:, 0:P])
                            ins = nc.vector.tensor_copy(PTt[0:NS, 13:15], src[0:NS, P:3 * P].rearrange(
                                "p (a q) -> p a q", q=P))
                        ins.then_inc(s_pk, 1)
                    dve.wait_ge(s_o, hi + 2)
                    nc.vector.tensor_copy(oS[:, :, hi].rearrange("p h b t -> p h b t"),
                                          OB[:, 0:P].rearrange("p (b h t) -> p h b t", b=4, h=H)).then_inc(s_ok, 1)
                dve.wait_ge(s_or, 1)
                for g in range(G):
                    nc.vector.tensor_copy(e.attn[0:NS, PT, g * R * HD:(g + 1) * R * HD], e.bank[5 + g][0:NS, 0:R * HD])

            def use(pe, hi, b4, q):
                j = 3 * (4 * hi + b4) + q
                pe.wait_ge(s_kk, j + 1)
                out = (SB[0], SB[1], WB)[q]
                nc.tensor.matmul(out[:], e.qpad[:, 4 * hi + b4], kT[:, (j % 4) // 2, j % 2 * 512:(j % 2 + 1) * 512],
                                 start=(b4 == 0), stop=(b4 == 3)).then_inc(s_ks, 1)

            @block.tensor
            def _(pe):
                pe.sem_inc(s_o, 1)
                for hi in range(2):
                    if hi:
                        pe.wait_ge(s_p, 3)
                    for b4 in range(4):
                        b = 4 * hi + b4
                        pe.wait_ge(s_selr[b4], 16 * PAGES * (hi + 1))
                        pe.wait_ge(s_winr[b4], 16 * (hi + 1))
                        for q in range(3):
                            j = 3 * b + q
                            if j >= 2:
                                pe.wait_ge(s_kk, j - 1)
                            if b4 == 0 and hi:
                                pe.wait_ge(s_pk, 4)
                            for i in range(4):
                                src = selr[:, b4, 4 * q + i, 0:P] if q < 2 else winr[:, b4, i, 0:P]
                                last = nc.tensor.transpose(e.bank[5 + j % 2][:, i * P:(i + 1) * P], src, e.ident)
                            last.then_inc(s_kt, 1)
                            if q:
                                use(pe, hi, b4, q - 1)
                        use(pe, hi, b4, 2)
                        nc.tensor.matmul(CB[:, 0:NC_S], e.qpad[:, b], e.kcT_s[:, b], start=(b4 == 0), stop=(b4 == 3))
                    nc.tensor.matmul(NBK[:, 0:NS], e.qall[:, hi], e.newT[:, 0], start=True, stop=True)
                    nc.tensor.matmul(NBK[:, NS:2 * NS], e.qall[:, hi], e.newT[:, 1], start=True,
                                     stop=True).then_inc(s_sc, 1)
                    pe.wait_ge(s_bs, hi + 1)
                    nc.tensor.matmul(NBK[:, 64:64 + NSEL], e.consts[:, C_SAME:C_SAME + P], blk[:], start=True,
                                     stop=True).then_inc(s_im, 1)
                    pe.wait_ge(s_p, 3 * hi + 3)
                    srcs = ([(pc[:, 1:1 + NC_S])] + [lsel[:, i * P:(i + 1) * P] for i in range(PAGES)]
                            + [lwin[:, i * P:(i + 1) * P] for i in range(4)] + [lsel[:, PAST:], lwin[:, WIN:]])
                    for a, src in enumerate(srcs):
                        q = a // 4
                        if a % 4 == 0 and q >= 2:
                            pe.wait_ge(s_pk, 4 * hi + q - 1)
                        n = src.shape[1]
                        ins = nc.tensor.transpose(e.bank[5 + q % 2][0:n, a % 4 * P:(a % 4 + 1) * P], src, e.ident)
                        if a % 4 == 3 or a == NT - 1:
                            ins.then_inc(s_pT, 1)
                    pe.wait_ge(s_pk, 4 * hi + 4)
                    if hi:
                        pe.wait_ge(s_ok, 1)
                    nc.tensor.matmul(OB[:, 0:P], e.z[0:NS, PT, VS:VS + P], PTt[0:NS, 13], start=True, stop=False)
                    nc.tensor.matmul(OB[:, 0:P], e.z[0:NS, PT, VW:VW + P], PTt[0:NS, 14], start=False, stop=False)
                    for b4 in range(4):
                        b = 4 * hi + b4
                        out = OB[:, b4 * 32:(b4 + 1) * 32]
                        cols = slice(b4 * 32, (b4 + 1) * 32)
                        nc.tensor.matmul(out, e.vc_s[:, b], PTt[0:NC_S, 0, cols], start=False, stop=False)
                        for i in range(PAGES):
                            nc.tensor.matmul(out, selr[:, b4, i, P:], PTt[:, 1 + i, cols], start=False, stop=False)
                        for i in range(4):
                            last = nc.tensor.matmul(out, winr[:, b4, i, P:], PTt[:, 9 + i, cols], start=False,
                                                    stop=(b4 == 3 and i == 3))
                    last.then_inc(s_o, 1)
                pe.wait_ge(s_ok, 2)
                for h in range(H):
                    lo = h // R * HD
                    last = nc.tensor.transpose(e.bank[5 + h // R][0:NS, h % R * HD:(h % R + 1) * HD],
                                               oS[lo:lo + HD, h].rearrange("p a b t -> p (a b t)"),
                                               e.ident[lo:lo + HD, lo:lo + HD])
                last.then_inc(s_or, 1)

def stage_mix(e):
    nc = e.nc
    with ExitStack() as ctx:
        w = e.sb("w_out_sb", [P, KD, D], ctx=ctx)
        catT = e.sb("mix_transposed", [P, 2, KD, P], ctx=ctx)
        xt = e.sb("x_again", [P, 2, D], ctx=ctx)
        gains = e.sb("mix_gains", [P, 4, CW], ctx=ctx)
        csm = e.sb("sample_conv", [P, 4, NS], ctx=ctx)
        tmp = e.tap[:].rearrange("p a n -> p (a n)")[:, 0:2 * CW].rearrange("p (a c) -> p a c", a=2)
        st = e.sb("mix_stats", [P, TILES, 8], ctx=ctx)
        conv = e.bias_p[:].rearrange("p a b -> p (a b)")[:, 0:TILES * CW].rearrange("p (i c) -> p i c", i=TILES)

        s_w = e.sem("w_out_loaded")
        s_g = e.sem("mix_gains_loaded")
        s_x = [e.sem(f"x_again_loaded{i}") for i in range(2)]
        s_cs = e.sem("sample_conv_compact")
        s_ct = e.sem("conv_rows_turned")
        s_cy = e.sem("conv_rows_kept")
        s_yc = e.sem("conv_rows_centred")
        s_sq = e.sem("mix_squares")
        s_vr = e.sem("mix_variances")
        s_rt = e.sem("mix_roots")
        s_ch = e.sem("mix_chain")
        s_cn = e.sem("conv_rows_normed")
        s_si = e.sem("conv_silu")
        s_ca = e.sem("mix_rows_ready")
        s_tt = e.sem("mix_turned")
        s_tk = e.sem("mix_turned_kept")
        s_mm = e.sem("mix_product")
        s_x1 = e.sem("first_residual")
        s_h2 = e.sem("h2_square")
        s_v2 = e.sem("h2_variance")
        s_r2 = e.sem("h2_root")
        s_hd = e.sem("h2_ready")
        x_of = [e.x_prompt[0, i * P:(i + 1) * P, :] for i in range(PT)] + [e.x_sample.rearrange("b t d -> (b t) d")]

        with nc.Block(no_gpsimd_drain=True) as block:
            @block.sync
            def _(sp):
                for a, g in enumerate((e.attn_out_norm, e.conv_ln_g, e.conv_ln_b, e.conv_out_scale)):
                    sp.dma_start(gains[:, a], g.to_broadcast([P, CW])).then_inc(s_g, 16)
                sp.dma_start(w[:], e.w_out[0].rearrange("(k p) n -> p k n", p=P)).then_inc(s_w, 16)
                for i in range(TILES):
                    if i >= 2:
                        sp.wait_ge(s_x1, i - 1)
                    sp.dma_start(xt[0:rows(i), i % 2], x_of[i]).then_inc(s_x[i % 2], 16)

            def square(act, i):
                r = rows(i)
                act.wait_ge(s_x1, i + 1)
                nc.scalar.activation(e.tap[0:r].rearrange("p a n -> p (a n)")[:, 0:D], e.x1[0:r, i], ACT.Square,
                                     accum_out=st[0:r, i, 4:5]).then_inc(s_h2, 1)
                act.wait_ge(s_v2, i + 1)
                nc.scalar.activation(st[0:r, i, 4:5], st[0:r, i, 4:5], ACT.Sqrt).then_inc(s_r2, 1)

            @block.scalar
            def _(act):
                for i in range(TILES):
                    r = rows(i)
                    act.wait_ge(s_ct, i + 1)
                    nc.scalar.activation(conv[0:r, i], e.bank[i % 2][0:r, :], ACT.Copy,
                                         accum_out=st[0:r, i, 0:1]).then_inc(s_cy, 1)
                    act.wait_ge(s_yc, i + 1)
                    nc.scalar.activation(tmp[0:r, 0], conv[0:r, i], ACT.Square, accum_out=st[0:r, i, 2:3])
                    nc.scalar.activation(tmp[0:r, 1], e.attn[0:r, i], ACT.Square,
                                         accum_out=st[0:r, i, 3:4]).then_inc(s_sq, 1)
                    act.wait_ge(s_vr, i + 1)
                    nc.scalar.activation(st[0:r, i, 2:4], st[0:r, i, 2:4], ACT.Sqrt).then_inc(s_rt, 1)
                for i in range(TILES):
                    r = rows(i)
                    act.wait_ge(s_cn, i + 1)
                    nc.scalar.activation(conv[0:r, i], conv[0:r, i], ACT.Silu).then_inc(s_si, 1)
                for i in range(TILES):
                    r = rows(i)
                    act.wait_ge(s_tt, i + 1)
                    if i >= 2:
                        act.wait_ge(s_mm, i - 1)
                    for q in range(2):
                        ins = nc.scalar.copy(catT[:, i % 2, 4 * q:4 * q + 4, 0:r],
                                             e.bank[2 * (i % 2) + q][:, 0:4 * r].rearrange("p (k n) -> p k n", k=4))
                    ins.then_inc(s_tk, 1)
                    if i >= 1:
                        square(act, i - 1)
                square(act, TILES - 1)

            @block.vector
            def _(dve):
                link = Chain(dve, s_ch)
                dve.wait_ge(e.s_conv, CK)
                nc.vector.tensor_copy(csm[:].rearrange("p c (b t) -> p c b t", b=NB),
                                      window(e.convo)).then_inc(s_cs, 1)
                dve.wait_ge(s_g, 64)
                for i in range(TILES):
                    r = rows(i)
                    dve.wait_ge(s_cy, i + 1)
                    link(nc.vector.tensor_scalar_mul(st[0:r, i, 1:2], st[0:r, i, 0:1], -1.0 / CW))
                    nc.vector.tensor_scalar_add(conv[0:r, i], conv[0:r, i], st[0:r, i, 1:2]).then_inc(s_yc, 1)
                    dve.wait_ge(s_sq, i + 1)
                    nc.vector.tensor_scalar(st[0:r, i, 2:4], st[0:r, i, 2:4], 1.0 / CW, EPS, ALU.mult,
                                            ALU.add).then_inc(s_vr, 1)
                    dve.wait_ge(s_rt, i + 1)
                    link(nc.vector.reciprocal(st[0:r, i, 2:4], st[0:r, i, 2:4]))
                    link(nc.vector.scalar_tensor_tensor(conv[0:r, i], conv[0:r, i], st[0:r, i, 2:3], gains[0:r, 1],
                                                        ALU.mult, ALU.mult))
                    nc.vector.scalar_tensor_tensor(e.attn[0:r, i], e.attn[0:r, i], st[0:r, i, 3:4], gains[0:r, 0],
                                                   ALU.mult, ALU.mult)
                    nc.vector.tensor_tensor(conv[0:r, i], conv[0:r, i], gains[0:r, 2], ALU.add).then_inc(s_cn, 1)
                for i in range(TILES):
                    r = rows(i)
                    dve.wait_ge(s_si, i + 1)
                    nc.vector.tensor_tensor(conv[0:r, i], conv[0:r, i], gains[0:r, 3], ALU.mult).then_inc(s_ca, 1)
                for i in range(TILES):
                    r, s = rows(i), int(i == PT)
                    dve.wait_ge(s_mm, i + 1)
                    for q in range(2):
                        c = slice(q * 512, (q + 1) * 512)
                        last = nc.vector.tensor_tensor(e.x1[0:r, i, c], e.bank[4 + 2 * (i % 2) + q][0:r, :],
                                                       e.mods[0:r, s, 0, c], ALU.mult)
                    link(last)
                    dve.wait_ge(s_x[i % 2], 16 * (i // 2 + 1))
                    nc.vector.tensor_tensor(e.x1[0:r, i], e.x1[0:r, i], xt[0:r, i % 2], ALU.add).then_inc(s_x1, 1)
                    dve.wait_ge(s_h2, i + 1)
                    nc.vector.tensor_scalar(st[0:r, i, 4:5], st[0:r, i, 4:5], 1.0 / D, EPS, ALU.mult,
                                            ALU.add).then_inc(s_v2, 1)
                    dve.wait_ge(s_r2, i + 1)
                    link(nc.vector.reciprocal(st[0:r, i, 4:5], st[0:r, i, 4:5]))
                    link(nc.vector.scalar_tensor_tensor(e.h2[0:r, i], e.x1[0:r, i], st[0:r, i, 4:5],
                                                        e.mods[0:r, s, 2], ALU.mult, ALU.mult))
                    nc.vector.tensor_tensor(e.h2[0:r, i], e.h2[0:r, i], e.mods[0:r, s, 1], ALU.add).then_inc(s_hd, 1)

            @block.tensor
            def _(pe):
                pe.wait_ge(s_cs, 1)
                for i in range(TILES):
                    r = rows(i)
                    if i >= 2:
                        pe.wait_ge(s_cy, i - 1)
                    for ct in range(4):
                        src = e.convo[:, ct, i * P:(i + 1) * P] if i < PT else csm[:, ct]
                        last = nc.tensor.transpose(e.bank[i % 2][0:r, ct * P:(ct + 1) * P], src, e.ident)
                    last.then_inc(s_ct, 1)
                pe.wait_ge(s_cy, TILES)
                pe.wait_ge(s_w, 16)

                def product(i):
                    r = rows(i)
                    pe.wait_ge(s_tk, i + 1)
                    if i >= 2:
                        pe.wait_ge(s_x1, i - 1)
                    for q in range(2):
                        for k in range(KD):
                            last = nc.tensor.matmul(e.bank[4 + 2 * (i % 2) + q][0:r, :], catT[:, i % 2, k, 0:r],
                                                    w[:, k, q * 512:(q + 1) * 512], start=(k == 0), stop=(k == KD - 1))
                    last.then_inc(s_mm, 1)

                for i in range(TILES):
                    r = rows(i)
                    pe.wait_ge(s_ca, i + 1)
                    if i >= 2:
                        pe.wait_ge(s_tk, i - 1)
                    for k in range(KD):
                        src = e.attn[0:r, i, k * P:(k + 1) * P] if k < 4 else conv[0:r, i, (k - 4) * P:(k - 3) * P]
                        last = nc.tensor.transpose(e.bank[2 * (i % 2) + k // 4][:, k % 4 * r:(k % 4 + 1) * r], src,
                                                   e.ident[0:r, 0:r])
                    last.then_inc(s_tt, 1)
                    if i >= 1:
                        product(i - 1)
                product(TILES - 1)


def window(convo):
    ap = convo[:]
    pstep = ap.ap[0][0]
    return bass.AP(ap.tensor, ap.offset + SEQW, [[pstep, P], [CONVO, 4], [SMPW, NB], [1, DT]])


def stage_route(e):
    nc = e.nc
    HC = 2 * PH
    QW = 256
    NQ = HC * P // QW
    with ExitStack() as ctx:
        h2T = e.sb("h2_transposed", [P, KD, TOK], ctx=ctx)
        wq = e.sb("peer_q_ring", [P, 3, KD, QW], ctx=ctx)
        qT = e.sb("peer_queries", [P, HC, TOK], ctx=ctx)
        kr = e.sb("key_rows", [P, 4, P], ctx=ctx)
        keysT = e.sb("keys_transposed", [P, HC, P], ctx=ctx)
        sc = e.sb("key_scores", [P, HC, NK], ctx=ctx)
        v = e.sb("half_top", [P, HC, TK], ctx=ctx)
        ix = e.sb("half_index", [P, HC, TK], U32, ctx=ctx)
        ixf = e.sb("half_index_f", [P, HC, TK], ctx=ctx)
        cand = e.sb("sums", [P, PH, TK, TK], ctx=ctx)
        hot = e.sb("one_hot", [P, PH, TK, TK], ctx=ctx)
        tv = e.sb("top_sums", [P, PH, TK], ctx=ctx)
        tp = e.sb("top_places", [P, PH, TK], U32, ctx=ctx)
        ab = e.sb("places_split", [P, 2, PH, TK], U32, ctx=ctx)
        abf = e.sb("places_split_f", [P, 2, PH, TK], ctx=ctx)
        sel = e.sb("picked_index", [P, 2, PH, TK], ctx=ctx)
        sm = e.sb("gate_sums", [P, PH], ctx=ctx)

        s_wq = [e.sem(f"peer_q_loaded{i}") for i in range(3)]
        s_kr = [e.sem(f"key_rows_loaded{i}") for i in range(4)]
        s_kt = e.sem("peer_keys_turned")
        s_kk = e.sem("peer_keys_kept")
        s_ht = e.sem("h2_turned")
        s_hk = e.sem("h2_turned_kept")
        s_q = e.sem("query_product")
        s_qk = e.sem("query_kept")
        s_s = e.sem("key_score_product")
        s_sk = e.sem("key_scores_kept")
        s_su = e.sem("key_scores_used")
        s_ch = e.sem("route_chain")
        s_sx = e.sem("gate_shifted")
        s_ex = e.sem("route_gate_exp")

        peer_q = e.peer_q[0].rearrange("(k p) n -> p k n", p=P)
        keys = e.peer_keys[0].rearrange("h c n d -> (h c) n d")

        with nc.Block(no_gpsimd_drain=True) as block:
            @block.sync
            def _(sp):
                for n in range(NQ):
                    if n >= 3:
                        sp.wait_ge(s_q, 2 * (n - 2))
                    sp.dma_start(wq[:, n % 3], peer_q[:, :, n * QW:(n + 1) * QW]).then_inc(s_wq[n % 3], 16)

            @block.scalar
            def _(act):
                for j in range(HC):
                    if j >= 4:
                        act.wait_ge(s_kt, j - 3)
                    act.dma_start(kr[:, j % 4], keys[j]).then_inc(s_kr[j % 4], 16)
                    if j % 4 == 3:
                        act.wait_ge(s_kt, j + 1)
                        nc.scalar.copy(keysT[:, j - 3:j + 1].rearrange("p a n -> p (a n)"),
                                       e.bank[4 + j // 4 % 2][:]).then_inc(s_kk, 1)
                for i in range(TILES):
                    act.wait_ge(s_ht, i + 1)
                    r = rows(i)
                    for q in range(2):
                        ins = nc.scalar.copy(h2T[:, 4 * q:4 * q + 4, i * P:i * P + r],
                                             e.bank[2 * (i % 2) + q][:, 0:4 * r].rearrange("p (k n) -> p k n", k=4))
                    ins.then_inc(s_hk, 1)
                for j in range(HC):
                    act.wait_ge(s_q, j + 1)
                    nc.scalar.copy(qT[:, j, 0:SEQ], e.bank[j % 2][:])
                    nc.scalar.copy(qT[:, j, SEQ:], e.bank[2 + j % 2][:, 0:NS]).then_inc(s_qk, 1)
                for i in range(TILES):
                    r = rows(i)
                    if i >= 1:
                        act.wait_ge(s_su, i)
                    for q in range(4):
                        act.wait_ge(s_s, 4 * i + q + 1)
                        nc.scalar.copy(sc[0:r, 4 * q:4 * q + 4].rearrange("p a n -> p (a n)"),
                                       e.bank[4 + q][0:r, :]).then_inc(s_sk, 1)
                    act.wait_ge(s_sx, i + 1)
                    nc.scalar.activation(e.gsm[0:r, i], e.gsm[0:r, i], ACT.Exp).then_inc(s_ex, 1)

            @block.vector
            def _(dve):
                link = Chain(dve, s_ch)

                def top16(r, n, src, vals, idx):
                    for j in range(n):
                        last = nc.vector.max(vals(j)[:, 0:8], src(j))
                    link(last)
                    for j in range(n):
                        nc.vector.max_index(idx(j)[:, 0:8], vals(j)[:, 0:8], src(j))
                    for j in range(n):
                        last = nc.vector.match_replace(src(j), vals(j)[:, 0:8], src(j), -3.0e38)
                    link(last)
                    for j in range(n):
                        last = nc.vector.max(vals(j)[:, 8:16], src(j))
                    link(last)
                    for j in range(n):
                        last = nc.vector.max_index(idx(j)[:, 8:16], vals(j)[:, 8:16], src(j))
                    return last

                iota = e.consts[:, C_IOTA:C_IOTA + TK]
                for i in range(TILES):
                    r = rows(i)
                    dve.wait_ge(s_sk, 4 * i + 4)
                    last = top16(r, HC, lambda j: sc[0:r, j], lambda j: v[0:r, j], lambda j: ix[0:r, j])
                    last.then_inc(s_su, 1)
                    dve.wait_ge(s_su, i + 1)
                    vv = v[0:r].rearrange("p (h c) k -> p h c k", c=2)
                    link(nc.vector.tensor_copy(ixf[0:r], ix[0:r]))
                    link(nc.vector.tensor_tensor(cand[0:r], span(vv[:, :, 0], 3, TK), span(vv[:, :, 1], 2, TK), ALU.add))
                    flat = cand[0:r].rearrange("p h a b -> p h (a b)")
                    link(top16(r, PH, lambda j: flat[:, j], lambda j: tv[0:r, j], lambda j: tp[0:r, j]))
                    nc.vector.tensor_single_scalar(ab[0:r, 0], tp[0:r], 4, ALU.logical_shift_right)
                    link(nc.vector.tensor_single_scalar(ab[0:r, 1], tp[0:r], 15, ALU.bitwise_and))
                    link(nc.vector.tensor_copy(abf[0:r], ab[0:r]))
                    ii = ixf[0:r].rearrange("p (h c) k -> p h c k", c=2)
                    for c in range(2):
                        wide = span(span(iota[0:r], 1, TK), 1, PH)
                        link(nc.vector.tensor_tensor(hot[0:r], span(abf[0:r, c], 3, TK), wide, ALU.is_equal))
                        link(nc.vector.tensor_tensor(hot[0:r], hot[0:r], span(ii[:, :, c], 2, TK), ALU.mult))
                        link(nc.vector.tensor_reduce(sel[0:r, c], hot[0:r], AX, ALU.add))
                    link(nc.vector.scalar_tensor_tensor(sel[0:r, 0], sel[0:r, 0], float(NK), sel[0:r, 1],
                                                        ALU.mult, ALU.add))
                    nc.vector.tensor_copy(e.eidx[0:r, i].rearrange("p (h k) -> p h k", h=PH), sel[0:r, 0])
                    gs = e.gsm[0:r, i].rearrange("p (h k) -> p h k", h=PH)
                    nc.vector.tensor_tensor(gs, tv[0:r], span(tv[0:r, :, 0], 2, TK), ALU.subtract).then_inc(s_sx, 1)
                    dve.wait_ge(s_ex, i + 1)
                    link(nc.vector.tensor_reduce(sm[0:r], gs, AX, ALU.add))
                    link(nc.vector.reciprocal(sm[0:r], sm[0:r]))
                    link(nc.vector.tensor_tensor(gs, gs, span(sm[0:r], 2, TK), ALU.mult))

            @block.tensor
            def _(pe):
                for j in range(HC):
                    pe.wait_ge(s_kr[j % 4], 16 * (j // 4 + 1))
                    if j % 4 == 0 and j >= 8:
                        pe.wait_ge(s_kk, j // 4 - 1)
                    nc.tensor.transpose(e.bank[4 + j // 4 % 2][:, j % 4 * P:(j % 4 + 1) * P], kr[:, j % 4],
                                        e.ident).then_inc(s_kt, 1)
                for i in range(TILES):
                    r = rows(i)
                    if i >= 2:
                        pe.wait_ge(s_hk, i - 1)
                    for k in range(KD):
                        last = nc.tensor.transpose(e.bank[2 * (i % 2) + k // 4][:, k % 4 * r:(k % 4 + 1) * r],
                                                   e.h2[0:r, i, k * P:(k + 1) * P], e.ident[0:r, 0:r])
                    last.then_inc(s_ht, 1)
                pe.wait_ge(s_hk, TILES)
                for j in range(HC):
                    n = j * P // QW
                    pe.wait_ge(s_wq[n % 3], 16 * (n // 3 + 1))
                    if j >= 2:
                        pe.wait_ge(s_qk, j - 1)
                    for o, m, b in ((0, SEQ, 0), (SEQ, NS, 2)):
                        for k in range(KD):
                            last = nc.tensor.matmul(e.bank[b + j % 2][:, 0:m],
                                                    wq[:, n % 3, k, j * P % QW:j * P % QW + P], h2T[:, k, o:o + m],
                                                    start=(k == 0), stop=(k == KD - 1))
                    last.then_inc(s_q, 1)
                pe.wait_ge(s_kk, 4)
                pe.wait_ge(s_qk, HC)
                for i in range(TILES):
                    r = rows(i)
                    for q in range(4):
                        if i >= 1:
                            pe.wait_ge(s_sk, 4 * (i - 1) + q + 1)
                        for a in range(4):
                            j = 4 * q + a
                            last = nc.tensor.matmul(e.bank[4 + q][0:r, a * P:(a + 1) * P], qT[:, j, i * P:i * P + r],
                                                    keysT[:, j], start=True, stop=True)
                        last.then_inc(s_s, 1)


def stage_experts(e):
    nc = e.nc
    RING = TK
    with ExitStack() as ctx:
        ring = e.sb("expert_rows", [P, RING, D], ctx=ctx)
        eb = e.sb("head_experts", [P, 2, TK], I32, ctx=ctx)
        dots = e.sb("head_dots", [P, 2, TK], ctx=ctx)
        act_v = e.sb("head_gelu", [P, 2, TK], ctx=ctx)
        wv = e.sb("head_weights", [P, 2, TK], ctx=ctx)
        diag = e.sb("weight_diagonals", [P, 4, P], ctx=ctx)
        zero = e.sb("zero_block", [P, P], ctx=ctx)
        yt = e.sb("y_tiles", [P, 2, D], ctx=ctx)

        s_buf = [e.sem(f"rows_landed{j}") for j in range(RING)]
        s_ix = e.sem("head_experts_ready")
        s_z = e.sem("zero_ready")
        s_u = e.sem("dots_done")
        s_go = e.sem("gathers_let_go")
        s_ga = e.sem("gelu_done")
        s_w = e.sem("weights_ready")
        s_d = e.sem("diagonals_ready")
        s_v = e.sem("buffers_free")
        s_acc = e.sem("tile_summed")
        s_ch = e.sem("experts_chain")
        s_y = e.sem("y_ready")
        s_yo = [e.sem(f"y_stored{j}") for j in range(2)]

        out_of = [e.y_prompt[0, i * P:(i + 1) * P, :] for i in range(PT)] + [e.y_sample.rearrange("b t d -> (b t) d")]
        eu, ev = e.expert_u[0], e.expert_v[0]

        with nc.Block() as block:
            @block.gpsimd
            def _(pool):
                for i in range(TILES):
                    r = rows(i)
                    with pool.Fori(0, PH // 2) as hb:
                        for p in range(2):
                            q = 2 * hb + (PH * i + p)
                            nc.gpsimd.tensor_copy(eb[0:r, p], e.eidx[0:r, i, bass.ds(hb * (2 * TK) + p * TK, TK)]
                                                  ).then_inc(s_ix, 1)
                            pool.wait_ge(s_ix, q + 1)
                            for j in range(TK):
                                pool.wait_ge(s_v, q * TK + (j + 1))
                                pool.sem_inc(s_go, 1)
                                pool.indirect_dma_start(ring[0:r, j], None, eu, bass.IndirectOffsetOnAxis(
                                    ap=eb[0:r, p, j:j + 1], axis=0)).then_inc(s_buf[j], 16)
                            for j in range(TK):
                                pool.wait_ge(s_u, q * TK + (j + 1))
                                pool.sem_inc(s_go, 1)
                                pool.indirect_dma_start(ring[0:r, j], None, ev, bass.IndirectOffsetOnAxis(
                                    ap=eb[0:r, p, j:j + 1], axis=0)).then_inc(s_buf[j], 16)

            @block.sync
            def _(sp):
                for i in range(TILES):
                    r = rows(i)
                    sp.wait_ge(s_y, i + 1)
                    sp.dma_start(out_of[i], yt[0:r, i % 2]).then_inc(s_yo[i % 2], 16)
                for j in range(2):
                    sp.wait_ge(s_yo[j], 16 * ((TILES + 1 - j) // 2))

            @block.scalar
            def _(act):
                for i in range(TILES):
                    r = rows(i)
                    with act.Fori(0, PH // 2) as hb:
                        for p in range(2):
                            q = 2 * hb + (PH * i + p)
                            act.wait_ge(s_u, q * TK + TK)
                            nc.scalar.activation(act_v[0:r, p], dots[0:r, p], ACT.Gelu_apprx_tanh).then_inc(s_ga, 1)
                            act.wait_ge(s_w, q + 1)
                            for j in range(TK):
                                act.wait_ge(s_v, q * TK + (RING + j - 3))
                                nc.scalar.activation(diag[:, j % 4], e.ident, ACT.Copy,
                                                     scale=wv[:, p, j:j + 1]).then_inc(s_d, 1)

            @block.vector
            def _(dve):
                link = Chain(dve, s_ch)
                nc.vector.memset(zero[:], 0.0).then_inc(s_z, 1)
                for i in range(TILES):
                    r, s = rows(i), int(i == PT)
                    with dve.Fori(0, PH // 2) as hb:
                        for p in range(2):
                            q = 2 * hb + (PH * i + p)
                            for j in range(TK):
                                dve.wait_ge(s_buf[j], q * 32 + 16)
                                nc.vector.tensor_tensor_reduce(
                                    out=ring[0:r, j], in0=ring[0:r, j], in1=e.h2[0:r, i], scale=1.0, scalar=0.0,
                                    op0=ALU.mult, op1=ALU.add, accum_out=dots[0:r, p, j:j + 1]).then_inc(s_u, 1)
                            dve.wait_ge(s_ga, q + 1)
                            nc.vector.tensor_tensor(wv[0:r, p], act_v[0:r, p],
                                                    e.gsm[0:r, i, bass.ds(hb * (2 * TK) + p * TK, TK)],
                                                    ALU.mult).then_inc(s_w, 1)
                    dve.wait_ge(s_acc, i + 1)
                    if i >= 2:
                        dve.wait_ge(s_yo[i % 2], 16 * (i // 2))
                    for c in range(2):
                        cs = slice(c * 512, (c + 1) * 512)
                        last = nc.vector.tensor_tensor(yt[0:r, i % 2, cs], e.bank[2 * (i % 2) + c][0:r, :],
                                                       e.mods[0:r, s, 3, cs], ALU.mult)
                    link(last)
                    nc.vector.tensor_tensor(yt[0:r, i % 2], yt[0:r, i % 2], e.x1[0:r, i], ALU.add).then_inc(s_y, 1)

            @block.tensor
            def _(pe):
                pe.wait_ge(s_z, 1)
                for i in range(TILES):
                    r = rows(i)
                    if i >= 2:
                        pe.wait_ge(s_y, i - 1)
                    acc = [e.bank[2 * (i % 2) + c][:] for c in range(2)]
                    for c in range(2):
                        last = nc.tensor.matmul(acc[c], zero[:], e.h2[:, 0, 0:512], start=True, stop=False)
                    if i == 0:
                        last.then_inc(s_v, RING)
                    with pe.Fori(0, PH // 2) as hb:
                        for p in range(2):
                            q = 2 * hb + (PH * i + p)
                            for j in range(TK):
                                pe.wait_ge(s_d, q * TK + (j + 1))
                                pe.wait_ge(s_buf[j], q * 32 + 32)
                                for c in range(2):
                                    last = nc.tensor.matmul(acc[c], diag[:, j % 4],
                                                            ring[:, j, c * 512:(c + 1) * 512],
                                                            start=False, stop=False)
                                last.then_inc(s_v, 1)
                    for c in range(2):
                        last = nc.tensor.matmul(acc[c], zero[:], e.h2[:, 0, 0:512], start=False, stop=True)
                    last.then_inc(s_acc, 1)

def build(nc, io):
    with ExitStack() as ctx:
        e = Env(nc, ctx, io)
        keep(e)
        e.mods = e.sb("mods", [P, 2, 4, D])
        region = e.sb("rows_region", [P, 2 * TILES * D])
        nz = TILES * ROWCOLS
        e.z = region[:, 0:nz].rearrange("p (i c) -> p i c", i=TILES)
        e.convu = region[:, nz:nz + 4 * CONVW].rearrange("p (c n) -> p c n", c=4)
        e.x1 = region[:, 0:TILES * D].rearrange("p (i d) -> p i d", i=TILES)
        e.h2 = region[:, TILES * D:].rearrange("p (i d) -> p i d", i=TILES)
        with ExitStack() as late:
            e.cw = e.sb("cw", [P, 4, CK + 1], ctx=late)
            e.bias_p = e.sb("bias_p", [P, H, SEQ], ctx=late)
            e.bias_s = e.sb("bias_s", [P, PAST], ctx=late)
            e.bias_w = e.sb("bias_w", [P, WIN], ctx=late)
            e.bias_n4 = e.sb("bias_n4", [P, DT], ctx=late)
            e.bias_new = e.sb("bias_new", [P, 2, NB, DT], ctx=late)
            e.gates = e.sb("gates", [P, TILES, 3 * H], ctx=late)
            e.gates_s = e.sb("gates_s", [P, 2, 3], ctx=late)
            with ExitStack() as early:
                e.mods1 = e.sb("mods1", [P, 2, 2, D], ctx=early)
                stage_ada(e)
                e.free_sems()
                stage_project(e)
                e.free_sems()
            e.qT = e.sb("qT", [P, PT, R, P], ctx=late)
            e.ksT = e.sb("ksT", [P, SEQ], ctx=late)
            e.kwT = e.sb("kwT", [P, SEQ], ctx=late)
            e.qpad = e.sb("qpad", [P, NB, P], ctx=late)
            e.qall = e.sb("qall", [P, 2, P], ctx=late)
            e.newT = e.sb("newT", [P, 2, NS], ctx=late)
            e.kcT_s = e.sb("kcT_s", [P, NB, NC_S], ctx=late)
            e.kcT_p = e.sb("kcT_p", [P, NC_P], ctx=late)
            e.vc_s = e.sb("vc_s", [NC_S, NB, P], ctx=late)
            e.vc_p = e.sb("vc_p", [NC_P, P], ctx=late)
            stage_qk(e)
            e.free_sems()
            stage_compress(e, 0)
            e.free_sems()
            stage_compress(e, 1)
            e.free_sems()
            e.attn = e.sb("attn", [P, TILES, AW], ctx=late)
            e.convo = e.sb("convo", [P, 4, CONVO], ctx=late)
            e.tap = e.sb("tap_products", [P, 2, CONVO], ctx=late)
            stage_prompt(e)
            stage_sample(e)
            stage_mix(e)
        e.eidx = e.sb("expert_index", [P, TILES, PH * TK], I32)
        e.gsm = e.sb("expert_gate", [P, TILES, PH * TK])
        stage_route(e)
        stage_experts(e)


OUTS = [
    ("y_prompt", (1, SEQ, D)), ("y_sample", (NB, DT, D)),
    ("new_cmp_prompt", (1, 1, SEQ, 2, G, HD)), ("new_sel_prompt", (1, 1, SEQ, 2, G, HD)),
    ("new_win_prompt", (1, 1, WIN, 2, G, HD)), ("new_conv_prompt", (1, 1, CK - 1, CW)),
    ("new_cmp_sample", (1, NB, DT, 2, G, HD)), ("new_sel_sample", (1, NB, DT, 2, G, HD)),
    ("new_win_sample", (1, NB, WIN, 2, G, HD)), ("new_conv_sample", (1, NB, CK - 1, CW)),
]


def kernel(**inputs):
    import concourse.bacc as bacc
    from concourse.bass_utils import run_bass_kernel_spmd

    consts, onehot = shape_constants()
    nc = bacc.Bacc("TRN2", target_bir_lowering=False, num_devices=1)
    arrays, io = {}, {}
    for name, a in {**inputs, "consts_in": consts, "onehot_in": onehot}.items():
        a = np.ascontiguousarray(a)
        arrays[f"in_{name}"] = a
        io[name] = nc.dram_tensor(f"in_{name}", a.shape, mybir.dt.from_np(a.dtype), kind="ExternalInput").ap()
    for name, shape in OUTS:
        io[name] = nc.dram_tensor(f"out_{name}", shape, F32, kind="ExternalOutput").ap()
    build(nc, io)
    r = run_bass_kernel_spmd(nc, [arrays], core_ids=[0])
    return tuple(r.results[0][f"out_{name}"] for name, _ in OUTS)
```
